# Optimizing a Trainium2 kernel written in Bass

```python
import math
import jax, jax.numpy as jnp
from jax import lax
import numpy as np
import jax
import jax.numpy as jnp

D_MODEL = 1024
BATCH = 1
SEQ = 256
DEPTH = 2

SSD_EXPAND = 2
SSD_D_INNER = SSD_EXPAND * D_MODEL
SSD_HEAD_DIM = 64
SSD_N_HEADS = SSD_D_INNER // SSD_HEAD_DIM
SSD_N_GROUPS = 4
SSD_HEADS_PER_GROUP = SSD_N_HEADS // SSD_N_GROUPS
SSD_D_STATE = 128
SSD_CONV_WIDTH = 4
SSD_CHUNK = 128
SSD_CONV_DIM = SSD_D_INNER + 2 * SSD_N_GROUPS * SSD_D_STATE

S5_WIDTH = D_MODEL
S5_GROUP = 16
S5_N_GROUPS = S5_WIDTH // S5_GROUP
S5_STATE = 64
S5_MIN_STEP = 0.001
S5_MAX_STEP = 0.1
S5_MAX_REAL = -1e-4

FFN_HIDDEN = 2816

RMS_EPS = 1e-6

IN_PROJ_DIM = SSD_D_INNER + SSD_CONV_DIM + SSD_N_HEADS + S5_WIDTH + 2 * D_MODEL
SPLITS = list(np.cumsum([SSD_D_INNER, SSD_CONV_DIM, SSD_N_HEADS, S5_WIDTH, D_MODEL]))


def rmsnorm(x, g):
    xf = x.astype(jnp.float32)
    xf = xf * lax.rsqrt(jnp.mean(xf * xf, axis=-1, keepdims=True) + RMS_EPS)
    return (xf * g.astype(jnp.float32)).astype(x.dtype)

def swiglu(x, w_gate, w_up, w_down):
    return (jax.nn.silu(x @ w_gate) * (x @ w_up)) @ w_down

def causal_depthwise_conv(u, w, b):
    k, c = w.shape
    out = lax.conv_general_dilated(
        u, w[:, None, :].astype(u.dtype), window_strides=(1,), padding=[(k - 1, 0)],
        dimension_numbers=("NWC", "WIO", "NWC"), feature_group_count=c)
    return out + b.astype(u.dtype)

def segsum(a):
    t = a.shape[-1]
    cs = jnp.cumsum(a, axis=-1)
    seg = cs[..., :, None] - cs[..., None, :]
    mask = jnp.tril(jnp.ones((t, t), dtype=bool))
    return jnp.where(mask, seg, -jnp.inf)

def ssd_chunked(xdt, adt, bmat, cmat):
    b, l, h, p = xdt.shape
    g, n = bmat.shape[2], bmat.shape[3]
    r = h // g
    q = SSD_CHUNK
    c = l // q
    X = xdt.reshape(b, c, q, g, r, p)
    A = adt.reshape(b, c, q, g, r).transpose(0, 3, 4, 1, 2)
    Bc = bmat.reshape(b, c, q, g, n)
    Cc = cmat.reshape(b, c, q, g, n)
    a_cum = jnp.cumsum(A, axis=-1)
    decay_in = jnp.exp(segsum(A))
    cb = jnp.einsum("bclgn,bcsgn->bcgls", Cc, Bc)
    y_diag = jnp.einsum("bcgls,bgrcls,bcsgrp->bclgrp", cb, decay_in, X)
    decay_states = jnp.exp(a_cum[..., -1:] - a_cum)
    states = jnp.einsum("bclgn,bgrcl,bclgrp->bcgrpn", Bc, decay_states, X)
    states = jnp.concatenate([jnp.zeros_like(states[:, :1]), states], axis=1)
    chunk_a = jnp.pad(a_cum[..., -1], ((0, 0), (0, 0), (0, 0), (1, 0)))
    chunk_decay = jnp.exp(segsum(chunk_a))
    new_states = jnp.einsum("bgrzc,bcgrpn->bzgrpn", chunk_decay, states)
    states = new_states[:, :-1]
    y_off = jnp.einsum("bclgn,bcgrpn,bgrcl->bclgrp", Cc, states, jnp.exp(a_cum))
    return (y_diag + y_off).reshape(b, l, h, p)

def ssd_branch(z, xbc, dt_raw, conv_w, conv_b, dt_bias, a_log, d_skip, norm_g):
    b, l, _ = z.shape
    xbc = jax.nn.silu(causal_depthwise_conv(xbc, conv_w, conv_b)).astype(jnp.float32)
    xs = xbc[..., :SSD_D_INNER].reshape(b, l, SSD_N_HEADS, SSD_HEAD_DIM)
    bm = xbc[..., SSD_D_INNER:SSD_D_INNER + SSD_N_GROUPS * SSD_D_STATE].reshape(b, l, SSD_N_GROUPS, SSD_D_STATE)
    cm = xbc[..., SSD_D_INNER + SSD_N_GROUPS * SSD_D_STATE:].reshape(b, l, SSD_N_GROUPS, SSD_D_STATE)
    dt = jax.nn.softplus(dt_raw.astype(jnp.float32) + dt_bias.astype(jnp.float32))
    a = -jnp.exp(a_log.astype(jnp.float32))
    y = ssd_chunked(xs * dt[..., None], a * dt, bm, cm) + d_skip.astype(jnp.float32)[:, None] * xs
    y = y.reshape(b, l, SSD_D_INNER)
    y = y * jax.nn.silu(z.astype(jnp.float32))
    yg = y.reshape(b, l, SSD_N_GROUPS, SSD_D_INNER // SSD_N_GROUPS)
    yg = yg * lax.rsqrt(jnp.mean(yg * yg, axis=-1, keepdims=True) + RMS_EPS)
    y = yg.reshape(b, l, SSD_D_INNER) * norm_g.astype(jnp.float32)
    return y.astype(z.dtype)

def s5_branch(u, lam_re, lam_im, b_re, b_im, c_re, c_im, log_step, d_skip, w_glu):
    b, l, _ = u.shape
    uf = u.astype(jnp.float32)
    ug = uf.reshape(b, l, S5_N_GROUPS, S5_GROUP)
    lam = lax.complex(jnp.minimum(lam_re.astype(jnp.float32), S5_MAX_REAL), lam_im.astype(jnp.float32))
    step = jnp.exp(log_step.astype(jnp.float32))[:, None]
    lam_bar = jnp.exp(lam * step)
    b_bar = ((lam_bar - 1.0) / lam)[..., None] * lax.complex(b_re.astype(jnp.float32), b_im.astype(jnp.float32))
    bu = jnp.einsum("blgc,gnc->blgn", ug.astype(jnp.complex64), b_bar)
    a_elems = jnp.broadcast_to(lam_bar, bu.shape)

    def combine(e1, e2):
        a1, s1 = e1
        a2, s2 = e2
        return a2 * a1, a2 * s1 + s2

    _, states = lax.associative_scan(combine, (a_elems, bu), axis=1)
    c = lax.complex(c_re.astype(jnp.float32), c_im.astype(jnp.float32))
    y = jnp.real(jnp.einsum("blgn,gcn->blgc", states, c)).reshape(b, l, S5_WIDTH)
    y = y + d_skip.astype(jnp.float32) * uf
    y = jax.nn.gelu(y).astype(u.dtype)
    val, gate = jnp.split(y @ w_glu, 2, axis=-1)
    return val * jax.nn.sigmoid(gate)

def mixer(u, w_in, ssd_conv_w, ssd_conv_b, ssd_dt_bias, ssd_a_log, ssd_d, ssd_norm_g, w_branch_a,
          s5_lambda_re, s5_lambda_im, s5_b_re, s5_b_im, s5_c_re, s5_c_im, s5_log_step, s5_d, s5_w_glu,
          w_branch_b, w_out):
    proj = u @ w_in
    z, xbc, dt_raw, u5, g_a, g_b = jnp.split(proj, SPLITS, axis=-1)
    y_a = ssd_branch(z, xbc, dt_raw, ssd_conv_w, ssd_conv_b, ssd_dt_bias, ssd_a_log, ssd_d, ssd_norm_g) @ w_branch_a
    y_b = s5_branch(u5, s5_lambda_re, s5_lambda_im, s5_b_re, s5_b_im, s5_c_re, s5_c_im,
                    s5_log_step, s5_d, s5_w_glu) @ w_branch_b
    merged = jax.nn.sigmoid(g_a) * y_a + jax.nn.sigmoid(g_b) * y_b
    return merged @ w_out

def first_inputs(seed: int = 0) -> dict:
    key = jax.random.key(seed)
    ks = iter(jax.random.split(key, 40))
    f32 = jnp.float32
    L = DEPTH

    def normal(shape, scale):
        return jax.random.normal(next(ks), shape, f32) * scale

    def gain(shape):
        return 1.0 + 0.02 * jax.random.normal(next(ks), shape, f32)

    x = jax.random.normal(next(ks), (BATCH, SEQ, D_MODEL), f32)
    d_ = D_MODEL
    dt_init = jnp.exp(jax.random.uniform(next(ks), (L, SSD_N_HEADS), f32,
                                         math.log(0.001), math.log(0.1)))
    n_idx = jnp.arange(S5_STATE, dtype=f32)
    return {
        "x": x,
        "ffn1_pre_g": gain((L, d_)),
        "ffn1_post_g": gain((L, d_)),
        "ffn1_w_gate": normal((L, d_, FFN_HIDDEN), d_ ** -0.5),
        "ffn1_w_up": normal((L, d_, FFN_HIDDEN), d_ ** -0.5),
        "ffn1_w_down": normal((L, FFN_HIDDEN, d_), FFN_HIDDEN ** -0.5),
        "mix_pre_g": gain((L, d_)),
        "mix_post_g": gain((L, d_)),
        "w_in": normal((L, d_, IN_PROJ_DIM), d_ ** -0.5),
        "ssd_conv_w": normal((L, SSD_CONV_WIDTH, SSD_CONV_DIM), SSD_CONV_WIDTH ** -0.5),
        "ssd_conv_b": normal((L, SSD_CONV_DIM), 0.02),
        "ssd_dt_bias": dt_init + jnp.log(-jnp.expm1(-dt_init)),
        "ssd_a_log": jnp.log(jax.random.uniform(next(ks), (L, SSD_N_HEADS), f32, 1.0, 16.0)),
        "ssd_d": gain((L, SSD_N_HEADS)),
        "ssd_norm_g": gain((L, SSD_D_INNER)),
        "w_branch_a": normal((L, SSD_D_INNER, d_), SSD_D_INNER ** -0.5),
        "s5_lambda_re": -0.5 + 0.01 * jax.random.normal(next(ks), (L, S5_N_GROUPS, S5_STATE), f32),
        "s5_lambda_im": math.pi * n_idx + 0.01 * jax.random.normal(next(ks), (L, S5_N_GROUPS, S5_STATE), f32),
        "s5_b_re": normal((L, S5_N_GROUPS, S5_STATE, S5_GROUP), (2 * S5_GROUP) ** -0.5),
        "s5_b_im": normal((L, S5_N_GROUPS, S5_STATE, S5_GROUP), (2 * S5_GROUP) ** -0.5),
        "s5_c_re": normal((L, S5_N_GROUPS, S5_GROUP, S5_STATE), (2 * S5_STATE) ** -0.5),
        "s5_c_im": normal((L, S5_N_GROUPS, S5_GROUP, S5_STATE), (2 * S5_STATE) ** -0.5),
        "s5_log_step": jax.random.uniform(next(ks), (L, S5_N_GROUPS), f32,
                                          math.log(S5_MIN_STEP), math.log(S5_MAX_STEP)),
        "s5_d": normal((L, S5_WIDTH), 1.0),
        "s5_w_glu": normal((L, S5_WIDTH, 2 * S5_WIDTH), S5_WIDTH ** -0.5),
        "w_branch_b": normal((L, S5_WIDTH, d_), S5_WIDTH ** -0.5),
        "w_out": normal((L, d_, d_), d_ ** -0.5),
        "ffn2_pre_g": gain((L, d_)),
        "ffn2_post_g": gain((L, d_)),
        "ffn2_w_gate": normal((L, d_, FFN_HIDDEN), d_ ** -0.5),
        "ffn2_w_up": normal((L, d_, FFN_HIDDEN), d_ ** -0.5),
        "ffn2_w_down": normal((L, FFN_HIDDEN, d_), FFN_HIDDEN ** -0.5),
    }

def first_block(x, ffn1_pre_g, ffn1_post_g, ffn1_w_gate, ffn1_w_up, ffn1_w_down,
              mix_pre_g, mix_post_g, w_in, ssd_conv_w, ssd_conv_b, ssd_dt_bias, ssd_a_log, ssd_d,
              ssd_norm_g, w_branch_a, s5_lambda_re, s5_lambda_im, s5_b_re, s5_b_im, s5_c_re, s5_c_im,
              s5_log_step, s5_d, s5_w_glu, w_branch_b, w_out,
              ffn2_pre_g, ffn2_post_g, ffn2_w_gate, ffn2_w_up, ffn2_w_down):
    h = x
    for i in range(DEPTH):
        f = swiglu(rmsnorm(h, ffn1_pre_g[i]), ffn1_w_gate[i], ffn1_w_up[i], ffn1_w_down[i])
        h = h + 0.5 * rmsnorm(f, ffn1_post_g[i])
        m = mixer(rmsnorm(h, mix_pre_g[i]), w_in[i], ssd_conv_w[i], ssd_conv_b[i], ssd_dt_bias[i],
                  ssd_a_log[i], ssd_d[i], ssd_norm_g[i], w_branch_a[i],
                  s5_lambda_re[i], s5_lambda_im[i], s5_b_re[i], s5_b_im[i], s5_c_re[i], s5_c_im[i],
                  s5_log_step[i], s5_d[i], s5_w_glu[i], w_branch_b[i], w_out[i])
        h = h + rmsnorm(m, mix_post_g[i])
        f = swiglu(rmsnorm(h, ffn2_pre_g[i]), ffn2_w_gate[i], ffn2_w_up[i], ffn2_w_down[i])
        h = h + 0.5 * rmsnorm(f, ffn2_post_g[i])
    return h


HEAD_DIM = 64
MIX_HEADS = 12
MIX_WIDTH = MIX_HEADS * HEAD_DIM
MEM_HEADS = 4
MEM_WIDTH = MEM_HEADS * HEAD_DIM
MEM_LEN = 256
CONV_WIDTH = 3
ROPE_DIM = HEAD_DIM // 4
ROPE_THETA = 500000.0
MOBA_BLOCK = 256
MOBA_TOPK = 3
MOBA_Q_CHUNK = 16
D_FF = 2816
N_EXPERTS = 8
TOP_K = 2
LN_EPS = 1e-5
N_A_LAYERS = DEPTH // 2
N_B_LAYERS = DEPTH - N_A_LAYERS
N_DENSE = (DEPTH + 1) // 2
N_MOE = DEPTH // 2
DEEPNORM_ALPHA = float((2 * DEPTH) ** 0.25)
DEEPNORM_BETA = float((8 * DEPTH) ** -0.25)
ATTN_SCALE = HEAD_DIM ** -0.5


def layer_norm(x, g, b):
    xf = x.astype(jnp.float32)
    mu = jnp.mean(xf, axis=-1, keepdims=True)
    var = jnp.mean(jnp.square(xf - mu), axis=-1, keepdims=True)
    y = (xf - mu) * lax.rsqrt(var + LN_EPS)
    return (y * g + b).astype(x.dtype)

def rope_tables(positions):
    inv_freq = ROPE_THETA ** (-jnp.arange(0, ROPE_DIM, 2, dtype=jnp.float32) / ROPE_DIM)
    angles = positions.astype(jnp.float32)[..., None] * inv_freq
    return jnp.cos(angles)[:, :, None, :], jnp.sin(angles)[:, :, None, :]

def apply_partial_rope(t, cos, sin):
    half = ROPE_DIM // 2
    t1 = t[..., :half].astype(jnp.float32)
    t2 = t[..., half:ROPE_DIM].astype(jnp.float32)
    rot = jnp.concatenate([t1 * cos - t2 * sin, t2 * cos + t1 * sin], axis=-1).astype(t.dtype)
    return jnp.concatenate([rot, t[..., ROPE_DIM:]], axis=-1)

def short_conv_mixer(u_b, u_c, u_h, conv_w):
    z = u_c * u_h
    z = lax.conv_general_dilated(
        z, conv_w[:, None, :], window_strides=(1,), padding=[(CONV_WIDTH - 1, 0)],
        dimension_numbers=('NWC', 'WIO', 'NWC'), feature_group_count=MIX_WIDTH)
    return u_b * z

def memory_cross_attention(q, k, v):
    logits = jnp.einsum('bshd,bmhd->bhsm', q, k).astype(jnp.float32) * ATTN_SCALE
    probs = jax.nn.softmax(logits, axis=-1).astype(v.dtype)
    out = jnp.einsum('bhsm,bmhd->bshd', probs, v)
    return out.reshape(q.shape[0], q.shape[1], -1)

def shared_key_value(h, w_kv, cos, sin):
    bsz, seq, _ = h.shape
    kv = jnp.einsum('bsd,de->bse', h, w_kv)
    k = apply_partial_rope(kv[..., :MIX_WIDTH].reshape(bsz, seq, MIX_HEADS, HEAD_DIM), cos, sin)
    v = kv[..., MIX_WIDTH:].reshape(bsz, seq, MIX_HEADS, HEAD_DIM)
    pad = (-seq) % MOBA_BLOCK
    k = jnp.pad(k, ((0, 0), (0, pad), (0, 0), (0, 0)))
    v = jnp.pad(v, ((0, 0), (0, pad), (0, 0), (0, 0)))
    n_blocks = (seq + pad) // MOBA_BLOCK
    k_blocks = k.reshape(bsz, n_blocks, MOBA_BLOCK, MIX_HEADS, HEAD_DIM).transpose(0, 3, 1, 2, 4)
    v_blocks = v.reshape(bsz, n_blocks, MOBA_BLOCK, MIX_HEADS, HEAD_DIM).transpose(0, 3, 1, 2, 4)
    k_means = jnp.mean(k_blocks.astype(jnp.float32), axis=3).astype(k.dtype)
    return k_blocks, v_blocks, k_means

def moba_attention(q, k_blocks, v_blocks, k_means):
    bsz, seq, n_heads, head_dim = q.shape
    n_blocks = k_blocks.shape[2]
    topk = min(MOBA_TOPK, n_blocks)
    n_sel = topk * MOBA_BLOCK
    n_chunks = seq // MOBA_Q_CHUNK
    q_chunks = q.reshape(bsz, n_chunks, MOBA_Q_CHUNK, n_heads, head_dim).transpose(1, 0, 3, 2, 4)
    b_idx = jnp.arange(bsz)[:, None, None, None]
    h_idx = jnp.arange(n_heads)[None, :, None, None]
    block_ids = jnp.arange(n_blocks)

    def one_chunk(args):
        c, qc = args
        start = c * MOBA_Q_CHUNK
        own = start // MOBA_BLOCK
        q_pos = start + jnp.arange(MOBA_Q_CHUNK)
        gate = jnp.einsum('bhqd,bhnd->bhqn', qc, k_means).astype(jnp.float32)
        gate = jnp.where(block_ids < own, gate, -jnp.inf)
        _, sel = lax.top_k(gate, topk)
        sel_valid = sel < own
        k_sel = k_blocks[b_idx, h_idx, sel]
        v_sel = v_blocks[b_idx, h_idx, sel]
        k_own = lax.dynamic_index_in_dim(k_blocks, own, axis=2, keepdims=False)
        v_own = lax.dynamic_index_in_dim(v_blocks, own, axis=2, keepdims=False)
        s_sel = jnp.einsum('bhqd,bhqkjd->bhqkj', qc, k_sel).astype(jnp.float32) * ATTN_SCALE
        s_sel = jnp.where(sel_valid[..., None], s_sel, -jnp.inf)
        s_own = jnp.einsum('bhqd,bhjd->bhqj', qc, k_own).astype(jnp.float32) * ATTN_SCALE
        k_pos = own * MOBA_BLOCK + jnp.arange(MOBA_BLOCK)
        s_own = jnp.where(k_pos[None, :] <= q_pos[:, None], s_own, -jnp.inf)
        scores = jnp.concatenate([s_sel.reshape(bsz, n_heads, MOBA_Q_CHUNK, n_sel), s_own], axis=-1)
        probs = jax.nn.softmax(scores, axis=-1).astype(qc.dtype)
        p_sel = probs[..., :n_sel].reshape(bsz, n_heads, MOBA_Q_CHUNK, topk, MOBA_BLOCK)
        p_own = probs[..., n_sel:]
        return (jnp.einsum('bhqkj,bhqkjd->bhqd', p_sel, v_sel)
                + jnp.einsum('bhqj,bhjd->bhqd', p_own, v_own))

    out = lax.map(one_chunk, (jnp.arange(n_chunks), q_chunks))
    return out.transpose(1, 0, 3, 2, 4).reshape(bsz, seq, n_heads * head_dim)

def swiglu_2(x, w_gu, w_down):
    gu = jnp.einsum('bsd,df->bsf', x, w_gu)
    g, u = gu[..., :D_FF], gu[..., D_FF:]
    return jnp.einsum('bsf,fd->bsd', jax.nn.silu(g) * u, w_down)

def moe_swiglu(x, w_router, w_gu, w_down):
    logits = jnp.einsum('bsd,de->bse', x, w_router).astype(jnp.float32)
    top_logits, top_idx = lax.top_k(logits, TOP_K)
    top_gates = jax.nn.softmax(top_logits, axis=-1)
    gates = jnp.sum(jax.nn.one_hot(top_idx, N_EXPERTS, dtype=jnp.float32) * top_gates[..., None], axis=-2)
    gates = gates.astype(x.dtype)
    out = jnp.zeros_like(x)
    for e in range(N_EXPERTS):
        out = out + gates[..., e:e + 1] * swiglu_2(x, w_gu[e], w_down[e])
    return out

def second_inputs(seed: int = 0) -> dict:
    key = jax.random.key(seed)
    ks = jax.random.split(key, 20)
    f32 = jnp.float32

    def nrm(k, shape, scale):
        return jax.random.normal(k, shape, f32) * scale

    x = nrm(ks[0], (BATCH, SEQ, D_MODEL), 1.0)
    mem = nrm(ks[1], (BATCH, MEM_LEN, D_MODEL), 1.0)
    offset = jax.random.randint(ks[2], (BATCH, 1), 0, 1024, dtype=jnp.int32)
    positions = offset + jnp.arange(SEQ, dtype=jnp.int32)[None, :]
    w_in_a = nrm(ks[3], (N_A_LAYERS, D_MODEL, 3 * MIX_WIDTH + MEM_WIDTH), D_MODEL ** -0.5)
    conv_a = nrm(ks[4], (N_A_LAYERS, CONV_WIDTH, MIX_WIDTH), CONV_WIDTH ** -0.5)
    w_q_b = nrm(ks[5], (N_B_LAYERS, D_MODEL, MIX_WIDTH + MEM_WIDTH), D_MODEL ** -0.5)
    w_kv_shared = nrm(ks[6], (D_MODEL, 2 * MIX_WIDTH), D_MODEL ** -0.5)
    w_mem_kv = nrm(ks[7], (DEPTH, D_MODEL, 2 * MEM_WIDTH), D_MODEL ** -0.5)
    w_o = nrm(ks[8], (DEPTH, MIX_WIDTH + MEM_WIDTH, D_MODEL), (MIX_WIDTH + MEM_WIDTH) ** -0.5 * DEEPNORM_BETA)
    ln1_g = 1.0 + nrm(ks[9], (DEPTH, D_MODEL), 0.02)
    ln1_b = nrm(ks[10], (DEPTH, D_MODEL), 0.02)
    ln2_g = 1.0 + nrm(ks[11], (DEPTH, D_MODEL), 0.02)
    ln2_b = nrm(ks[12], (DEPTH, D_MODEL), 0.02)
    w_gu_dense = nrm(ks[13], (N_DENSE, D_MODEL, 2 * D_FF), D_MODEL ** -0.5)
    w_down_dense = nrm(ks[14], (N_DENSE, D_FF, D_MODEL), D_FF ** -0.5 * DEEPNORM_BETA)
    w_router = nrm(ks[15], (N_MOE, D_MODEL, N_EXPERTS), D_MODEL ** -0.5)
    w_gu_moe = nrm(ks[16], (N_MOE, N_EXPERTS, D_MODEL, 2 * D_FF), D_MODEL ** -0.5)
    w_down_moe = nrm(ks[17], (N_MOE, N_EXPERTS, D_FF, D_MODEL), D_FF ** -0.5 * DEEPNORM_BETA)
    return {'x': x, 'mem': mem, 'positions': positions, 'w_in_a': w_in_a, 'conv_a': conv_a,
            'w_q_b': w_q_b, 'w_kv_shared': w_kv_shared, 'w_mem_kv': w_mem_kv, 'w_o': w_o,
            'ln1_g': ln1_g, 'ln1_b': ln1_b, 'ln2_g': ln2_g, 'ln2_b': ln2_b,
            'w_gu_dense': w_gu_dense, 'w_down_dense': w_down_dense, 'w_router': w_router,
            'w_gu_moe': w_gu_moe, 'w_down_moe': w_down_moe}

def second_block(x, mem, positions, w_in_a, conv_a, w_q_b, w_kv_shared, w_mem_kv, w_o,
              ln1_g, ln1_b, ln2_g, ln2_b, w_gu_dense, w_down_dense, w_router,
              w_gu_moe, w_down_moe):
    bsz, seq, _ = x.shape
    cos, sin = rope_tables(positions)
    shared = None
    for layer in range(DEPTH):
        mem_kv = jnp.einsum('bmd,de->bme', mem, w_mem_kv[layer])
        mem_k = mem_kv[..., :MEM_WIDTH].reshape(bsz, -1, MEM_HEADS, HEAD_DIM)
        mem_v = mem_kv[..., MEM_WIDTH:].reshape(bsz, -1, MEM_HEADS, HEAD_DIM)
        if layer < N_A_LAYERS:
            proj = jnp.einsum('bsd,de->bse', x, w_in_a[layer])
            u_b = proj[..., :MIX_WIDTH]
            u_c = proj[..., MIX_WIDTH:2 * MIX_WIDTH]
            u_h = proj[..., 2 * MIX_WIDTH:3 * MIX_WIDTH]
            q_mem = proj[..., 3 * MIX_WIDTH:]
            main = short_conv_mixer(u_b, u_c, u_h, conv_a[layer])
        else:
            proj = jnp.einsum('bsd,de->bse', x, w_q_b[layer - N_A_LAYERS])
            q = apply_partial_rope(proj[..., :MIX_WIDTH].reshape(bsz, seq, MIX_HEADS, HEAD_DIM), cos, sin)
            q_mem = proj[..., MIX_WIDTH:]
            k_blocks, v_blocks, k_means = shared
            main = moba_attention(q, k_blocks, v_blocks, k_means)
        mem_out = memory_cross_attention(q_mem.reshape(bsz, seq, MEM_HEADS, HEAD_DIM), mem_k, mem_v)
        mix = jnp.einsum('bse,ed->bsd', jnp.concatenate([main, mem_out], axis=-1), w_o[layer])
        x = layer_norm(DEEPNORM_ALPHA * x + mix, ln1_g[layer], ln1_b[layer])
        if layer % 2 == 0:
            ffn = swiglu_2(x, w_gu_dense[layer // 2], w_down_dense[layer // 2])
        else:
            ffn = moe_swiglu(x, w_router[layer // 2], w_gu_moe[layer // 2], w_down_moe[layer // 2])
        x = layer_norm(DEEPNORM_ALPHA * x + ffn, ln2_g[layer], ln2_b[layer])
        if layer == N_A_LAYERS - 1:
            shared = shared_key_value(x, w_kv_shared, cos, sin)
    return x


def setup_inputs(seed=0):
    out = dict(first_inputs(seed))
    for name, value in second_inputs(seed + 1).items():
        if name != "x":
            out[name + "_2"] = value
    return out


def reference(
    x, ffn1_pre_g, ffn1_post_g, ffn1_w_gate, ffn1_w_up, ffn1_w_down, mix_pre_g, mix_post_g,
    w_in, ssd_conv_w, ssd_conv_b, ssd_dt_bias, ssd_a_log, ssd_d, ssd_norm_g, w_branch_a,
    s5_lambda_re, s5_lambda_im, s5_b_re, s5_b_im, s5_c_re, s5_c_im, s5_log_step, s5_d, s5_w_glu,
    w_branch_b, w_out, ffn2_pre_g, ffn2_post_g, ffn2_w_gate, ffn2_w_up, ffn2_w_down, mem_2,
    positions_2, w_in_a_2, conv_a_2, w_q_b_2, w_kv_shared_2, w_mem_kv_2, w_o_2, ln1_g_2,
    ln1_b_2, ln2_g_2, ln2_b_2, w_gu_dense_2, w_down_dense_2, w_router_2, w_gu_moe_2,
    w_down_moe_2,
):
    x = first_block(
        x, ffn1_pre_g, ffn1_post_g, ffn1_w_gate, ffn1_w_up, ffn1_w_down, mix_pre_g, mix_post_g,
        w_in, ssd_conv_w, ssd_conv_b, ssd_dt_bias, ssd_a_log, ssd_d, ssd_norm_g, w_branch_a,
        s5_lambda_re, s5_lambda_im, s5_b_re, s5_b_im, s5_c_re, s5_c_im, s5_log_step, s5_d,
        s5_w_glu, w_branch_b, w_out, ffn2_pre_g, ffn2_post_g, ffn2_w_gate, ffn2_w_up,
        ffn2_w_down,
    )
    return second_block(
        x, mem_2, positions_2, w_in_a_2, conv_a_2, w_q_b_2, w_kv_shared_2, w_mem_kv_2, w_o_2,
        ln1_g_2, ln1_b_2, ln2_g_2, ln2_b_2, w_gu_dense_2, w_down_dense_2, w_router_2,
        w_gu_moe_2, w_down_moe_2,
    )


_drawn_inputs = setup_inputs


def setup_inputs(seed=0):
    import zlib

    import numpy as np

    out = dict(_drawn_inputs(seed))
    spreads = {}
    factors = {'s5_lambda_re': 200.0,
     'ffn2_post_g': 2.894,
     's5_lambda_im': 22.128,
     's5_b_re': 32.28,
     's5_b_im': 29.122,
     's5_c_re': 30.408,
     's5_c_im': 27.168,
     's5_log_step': 24.528}
    for name, (base, spread) in spreads.items():
        noise = np.random.default_rng([zlib.crc32(name.encode()), seed]).standard_normal(out[name].shape)
        drawn = base * np.exp(spread * noise) if base else spread * noise
        out[name] = jnp.asarray(drawn.astype(out[name].dtype))
    for name, factor in factors.items():
        out[name] = (out[name] * factor).astype(out[name].dtype)
    return out
```

```python
from collections import defaultdict
from contextlib import ExitStack, contextmanager

import numpy as np
import concourse.bass as bass
from concourse import mybir

F32 = mybir.dt.float32
F32R = mybir.dt.float32r
BF16 = mybir.dt.bfloat16
I32 = mybir.dt.int32
ALU = mybir.AluOpType
ACT = mybir.ActivationFunctionType
AX_X = mybir.AxisListType.X
MULT, ADD, SUB, MIN, MAX, EQ = ALU.mult, ALU.add, ALU.subtract, ALU.min, ALU.max, ALU.is_equal

P = 128
T = 256
D = 1024
DT = D // P
DEPTH = 2
HID = 2816
STEPS = HID // 256
N_EXPERTS = 8
SLOTS = 128
INNER = 2048
HEADS = 32
GROUPS = 4
S5_PAIRS = 32
RING = 3
RMS_EPS = 1e-6
LN_EPS = 1e-5
S5_MAX_REAL = -1e-4
ALPHA = float((2 * DEPTH) ** 0.25)
ATTN_SCALE = 64 ** -0.5
TWO_PI_HI = 6.28125
TWO_PI_LO = 2 * np.pi - 6.28125
PI_BELOW = 3.1415925
HALF_PI = float(np.pi / 2)
ROUND = 1.5 * 2.0 ** 23
LN2_HI, LN2_LO = 0.693359375, -2.12194440e-4

FFN1 = 0
MIX = FFN1 + 3 * STEPS
C_U5, C_DT, C_XBC, C_GATE, C_Z = MIX, MIX + 4, MIX + 5, MIX + 17, MIX + 25
C_A = C_Z + 8
C_G = C_A + 8
GLU_ORDER = [("v", 0), ("g", 0), ("v", 1), ("g", 1), ("b", 0), ("v", 2), ("g", 2), ("b", 1),
             ("v", 3), ("g", 3), ("b", 2), ("b", 3)]
C_OUT = C_G + len(GLU_ORDER)
FFN2 = C_OUT + 4
LAYER = FFN2 + 3 * STEPS
assert LAYER % RING == 0 and FFN2 % RING == 0
B_MEM, B_INA = 0, 4
B_WO1 = B_INA + 10
B_FFN = B_WO1 + 4
B_KV = B_FFN + 3 * STEPS
B_Q = B_KV + 6
B_WO2 = B_Q + 4
B_MOE = B_WO2 + 4
assert B_FFN % RING == 0
MOE_SLOTS = [(B_MOE + i) % RING for i in range(3)]
ROWS2 = 4 * DEPTH * DT + 18

CONST = {}


def _layout():
    at = 0
    for name, n in (("ident", 128), ("ones", 128), ("tri", 384), ("before", 128), ("iota", 256),
                    ("bmask", 2), ("cmask", 2), ("swap", 128), ("freq", 1), ("first", 8)):
        CONST[name] = (at, n)
        at += n
    return at


CONST_COLS = _layout()


def constants():
    p = np.arange(P)
    c = np.zeros((P, CONST_COLS), np.float32)

    def put(name, a):
        at, n = CONST[name]
        c[:, at:at + n] = a

    put("ident", np.eye(P))
    put("ones", 1.0)
    keep = (np.arange(256)[None, :] >= p[:, None]).astype(np.float32)
    put("tri", np.concatenate([keep, keep[:, :128]], 1))
    put("before", (p[:, None] < p[None, :]))
    put("iota", np.arange(256)[None, :])
    put("bmask", (p[:, None] // 64 == np.arange(2)[None, :]))
    put("cmask", ((p[:, None] // 16) % 2 == np.arange(2)[None, :]))
    swap = np.zeros((P, P), np.float32)
    freq = np.zeros((P, 1), np.float32)
    inv = (np.float32(500000.0) ** (-np.arange(0, 16, 2, dtype=np.float32) / np.float32(16))).astype(np.float32)
    for h in (0, 64):
        for i in range(8):
            swap[h + 8 + i, h + i] = -1.0
            swap[h + i, h + 8 + i] = 1.0
            freq[h + i] = freq[h + 8 + i] = inv[i]
    put("swap", swap)
    put("freq", freq)
    put("first", (N_EXPERTS - np.arange(N_EXPERTS))[None, :])
    return c


def causal_mask():
    return np.where(np.arange(T)[None, :] <= np.arange(T)[:, None], 0.0, -1e30).astype(np.float32)


PER = {
    "step": {
        "weights_ready": 3, "staged": 2, "chunk_used": 3, "gate_a": 1, "up_a": 1, "raw_a": 16, "raw_b": 16,
        "raw_c": 16, "hi_ready": 3, "silu_done": 2, "dve_step": 2},
    "layer": {
        "weights_ready": 123, "h_ready": 3, "params_in": 320, "squared": 6, "prm_ready": 1, "x_ready": 8,
        "staged": 76, "c_evicted": 41, "s5_ready": 1, "mats_masked": 8, "mats_ready": 8, "modulated": 32,
        "cproj_ready": 8, "h5_ready": 32, "y5_added": 8, "dt_rows_ready": 1, "silu_conv": 12, "dtok_ready": 1,
        "decay_ready": 32, "xt_ready": 8, "masked": 32, "gm_ready": 4, "y_ready": 16, "group_sq": 4, "acc_read":
        2, "chunk_used": 123, "prm_psum": 1, "summed": 6, "gate_a": 22, "up_a": 22, "s5_psum": 1, "mats_psum":
        8, "bu_done": 32, "y5_psum": 32, "dtok_psum": 1, "gm_psum": 4, "cum_psum": 16, "xt_psum": 8, "y_psum":
        16, "group_sum": 4, "raw_a": 656, "raw_b": 656, "raw_c": 656, "xf_ready": 6, "s5_step": 2,
        "turns_ready": 32, "dt_step": 2, "g_ready": 32, "tap_done": 12, "hi_ready": 123, "rooted": 6,
        "xh_ready": 8, "silu_done": 44, "s5_exp": 2, "act_step": 65, "table_ready": 32, "dt_act": 2, "y5_done":
        8, "group_root": 4, "dve_step": 216, "s5c_ready": 1, "bu_read": 32, "pool_step": 184},
    "moe_step": {
        "weights_ready": 3, "staged": 1, "hidden_ready": 1, "chunk_used": 3, "hidden_turned": 1, "raw_a": 16,
        "raw_b": 16, "raw_c": 16, "hi_ready": 3, "silu_done": 1, "kh_ready": 1},
    "expert": {
        "weights_ready": 33, "x_ready": 2, "staged": 11, "picked": 1, "scatter_ready": 1, "sum_added": 2,
        "hidden_ready": 11, "y_copied": 1, "chunk_used": 33, "gathered": 1, "scatter_turned": 1,
        "hidden_turned": 11, "scattered": 2, "raw_a": 176, "raw_b": 176, "raw_c": 176, "hi_ready": 33,
        "xh_ready": 2, "silu_done": 11, "kh_ready": 11, "dve_step": 1},
    "pass": {
        "weights_ready": 264, "x_ready": 16, "staged": 88, "picked": 8, "scatter_ready": 8, "sum_added": 16,
        "hidden_ready": 88, "y_copied": 8, "chunk_used": 264, "gathered": 8, "scatter_turned": 8,
        "hidden_turned": 88, "scattered": 16, "raw_a": 1408, "raw_b": 1408, "raw_c": 1408, "hi_ready": 264,
        "xh_ready": 16, "silu_done": 88, "kh_ready": 88, "dve_step": 9},
}


class Count:

    def __init__(self):
        self.seen = defaultdict(int)
        self.given = defaultdict(int)
        self.loops = []

    def _value(self, kind, name):
        v = kind[name]
        for reg, where in self.loops:
            per = PER.get(where, {}).get(name, 0)
            if per:
                v = reg * per + v
        return v

    def due(self, name, n=1):
        self.seen[name] += n
        return self._value(self.seen, name)

    def one(self, name):
        self.given[name] += 1
        return 1

    def peek(self, name, n=1):
        v = self.due(name, n)
        self.seen[name] -= n
        return v

    def last(self, name):
        return self._value(self.given, name)

    @contextmanager
    def loop(self, eng, n, where):
        before = [dict(k) for k in (self.seen, self.given)]
        with eng.Fori(0, n) as i:
            self.loops.append((i, where))
            yield i
            self.loops.pop()
        for k, old in zip((self.seen, self.given), before):
            for name in list(k):
                delta = k[name] - old.get(name, 0)
                if delta:
                    assert PER[where].get(name) == delta, (where, name, delta)
                    if isinstance(n, int):
                        k[name] += delta * (n - 1)
        if not isinstance(n, int):
            self.loops.append((n - 1, where))


TICKS = [("u", i) for i in range(4)] + [("d", 0)] + [("x", i) for i in range(12)] \
    + [("g", i) for i in range(8)] + [("z", i) for i in range(8)]
S5_STEPS = S5_PAIRS + 3
S5_AT = {k: [] for k in range(len(TICKS))}
for _q in range(S5_STEPS):
    S5_AT[5 + _q * 20 // S5_STEPS].append(_q)


def build(nc, a, out):
    ctx = ExitStack()
    with ctx:
        def sb(name, shape, dt=F32):
            return ctx.enter_context(nc.sbuf_tensor(name, shape, dt))

        raw = sb("raw", [P, RING, 2048])
        w_hi = sb("w_hi", [P, RING, 2048], F32R)
        w_lo = sb("w_lo", [P, RING, 2048], F32R)
        H = sb("H", [P, DT, T])
        x_hi = sb("x_hi", [P, DT, T], F32R)
        x_lo = sb("x_lo", [P, DT, T], F32R)
        k_hi = sb("k_hi", [P, 4, T], F32R)
        k_lo = sb("k_lo", [P, 4, T], F32R)
        stage = sb("stage", [P, 2, T])
        act_out = sb("act_out", [P, 2, T])
        XC = sb("XC", [P, 24, T])
        U5 = sb("U5", [P, DT, T])
        G = sb("G", [P, 16, T])
        conv_in = sb("conv_in", [P, 2, 2, T + 3])
        conv_out = sb("conv_out", [P, 2, 2, T])
        work = sb("work", [P, 7680])
        con = sb("con", [P, CONST_COLS])
        prm = sb("prm", [P, 192])
        s5_small = sb("s5_small", [32, 4])
        s5c = sb("s5c", [P, 7, 32])
        head_rows = sb("head_rows", [32, 4])
        rows = sb("rows", [P, 5, T])
        dt_tok = sb("dt_tok", [P, 5, 32])
        rstd = sb("rstd", [P, T])
        eps = sb("eps", [P, 3])
        zero_bf = sb("zero_bf", [1, P], BF16)

        PS = ctx.enter_context(nc.psum_tensor("PS", [P, 8, 512], F32))
        ACC = PS[:, 0:4, :].rearrange("p b (u n) -> p (b u) n", u=2)
        ACC_FLAT = PS[:, 0:4, :].rearrange("p b n -> p (b n)")

        def cst(name, rows=P, lo=0, n=None):
            at, width = CONST[name]
            return con[0:rows, at + lo:at + (lo + n if n else width)]

        def wk(at, *shape):
            n = int(np.prod(shape))
            v = work[:, at:at + n]
            names = "abc"[:len(shape)]
            return v.rearrange(f"p ({' '.join(names)}) -> p {' '.join(names)}", **dict(zip(names, shape))) if len(shape) > 1 else v

        squares = wk(0, DT, T)
        merged = wk(2048, DT, T)
        group_rstd = wk(0, 4, T)
        group_squares = [wk(4864, 4, T), wk(5888, 4, T)]
        zbuf = [conv_out[:, 0], conv_out[:, 1], act_out[:, :, :]]
        glu_gate = conv_in[:, :, :, 3:T + 3]
        prm_rows = XC[:, 22, :].rearrange("p (a n) -> p a n", a=2)
        s5_rows = XC[0:32, 20, :].rearrange("p (a n) -> p a n", a=2)
        rope_cos, rope_sin = rows[:, 0, :], rows[:, 1, :]
        causal = rows[:, 2:4, :]
        positions = XC[:, 21, :]
        router = prm[:, 96:160].rearrange("p (k e) -> p k e", k=DT)
        gated = work[:, 0:6 * (T + 2)].rearrange("p (k n) -> p k n", k=6)
        tapped = wk(2048, 6, T)
        probs = wk(4096, 2, 2 * T).rearrange("p b (t n) -> p b t n", t=2)
        probs_t = wk(5120, 2, 2 * T).rearrange("p b (t n) -> p b t n", t=2)
        att_small = wk(6144, 2, 6)
        rope_a, rope_b = wk(6400, T), wk(6656, T)
        rt = wk(6912, 10, 2, N_EXPERTS + 1)
        slot_of, gate_of = rt[:, 0], rt[:, 1]
        lg, top1, top2, rest, chosen = (rt[:, i, :, 0:N_EXPERTS] for i in (2, 3, 4, 5, 6))
        rsm = wk(7424, 12, 2)
        n_pass = work[:, 7460:7461]
        cur = work[:, 7464:7468]
        pick = wk(4096, 4, P)
        scatter = wk(4608, T)
        y_exp = wk(5120, 2 * 512)
        moe_sum = U5
        v_all = XC[:, 14:20, :].rearrange("p (t k) n -> p t (k n)", t=2)
        mem_heads = lambda l, q0: [(XC[:, q0 + j // 2, :], G[:, 2 * l + j // 2, :], G[:, 4 + 2 * l:6 + 2 * l, :], 64 * j,
                                    XC[:, 6 + j // 2, :], False) for j in range(4)]
        heads_a = mem_heads(0, 18)
        heads_b = [(XC[:, j // 2, :], XC[:, 8 + j // 2, :], v_all, 64 * j, XC[:, j // 2, :], True) for j in range(12)] \
            + mem_heads(1, 6)
        rope_tiles = [*range(6), *range(8, 14)]
        x_tok = XC[:, 0:8, :].rearrange("p (t k) n -> p t (k n)", t=2)
        m1, m2 = wk(0, 2, T), wk(512, 2, T)
        g5 = wk(1024, 2, 2 * T)
        damp_c, damp_s = wk(2048, 2, T), wk(2560, 2, T)
        h5 = wk(3072, 2, T)
        cos_t, sin_t = wk(3584, 3, T), wk(4352, 3, T)
        turns = wk(5120, 3, T)
        mats_in = wk(5888, 4, P)
        mats = wk(6400, 4, P)
        cproj = wk(6912, 2, 2 * P)
        cpt = wk(7424, 2, P)
        dt_rows = rows[0:32]
        s5row = work[0:32, 0:2304].rearrange("p (a n) -> p a n", n=P)
        decay = wk(0, 2, 4 * 384).rearrange("p b (h n) -> p b h n", h=4)
        gmask = wk(3072, 2, 384)
        xt = wk(3840, 2, 2 * T)
        b_raw = G[:, 8:12, :].rearrange("p k n -> p (k n)").rearrange("p (r q c) -> p r q c", r=2, c=16)
        c_raw = G[:, 12:16, :].rearrange("p k n -> p (k n)").rearrange("p (r q n) -> p r q n", r=2, n=64)

        names = ("raw_a raw_b raw_c hi_ready weights_ready chunk_used consts_in x_in params_in params_done "
                 "prm_psum prm_ready setup_done x_turned h_ready squared summed rooted xf_ready xh_ready x_ready "
                 "gate_a up_a silu_done staged c_evicted bu_read tap_done silu_conv mats_masked mats_psum mats_ready cproj_ready "
                 "turns_ready table_ready bu_done modulated g_ready h5_ready y5_psum y5_added y5_done "
                 "s5_exp s5_step s5_psum s5_ready s5c_ready dt_step dt_act dt_rows_ready dtok_psum dtok_ready "
                 "gm_psum gm_ready xt_psum xt_ready cum_psum decay_ready masked y_psum y_ready "
                 "group_sq group_sum group_root group_ready acc_read glu_ready "
                 "params2_in mem_in centered att_scores att_max att_exp att_norm att_turned att_copied att_out att_evicted "
                 "rope_ang rope_table rope_psum roped mixed logits gate_diff route_exp masks_ready ranks routed "
                 "picked gathered scattered scatter_turned scatter_ready hidden_ready hidden_turned kh_ready y_copied sum_added normed mean_sum tokens_turned tokens_ready "
                 "act_step dve_step pool_step pool_waited sp_waited out_turned out_ready out_sent").split()
        s = {n: ctx.enter_context(nc.semaphore(n)) for n in names}
        LANDED = ("raw_a", "raw_b", "raw_c")
        block = ctx.enter_context(nc.Block())

        def chunk_c(w, col, n=256):
            return w[:, col:col + n].rearrange("(k p) n -> p k n", p=P)

        def chunk_r(w, row):
            return w[row:row + 256, :].rearrange("(k p) n -> p k n", p=P)

        @block.sync
        def _(sp):
            n = Count()

            def load(slot, src, cols=2048, alone=False):
                sp.wait_ge(s["weights_ready"], n.due("weights_ready"))
                if alone:
                    sp.sem_inc(s["sp_waited"], 1)
                sp.dma_start(raw[:, slot, 0:cols].rearrange("p (k n) -> p k n", k=src.shape[1]), src)\
                  .then_inc(s[LANDED[slot]], 16)

            def ffn_step(gate, up, down, at):
                load(0, gate[:, bass.ds(at, 256)].rearrange("(k p) n -> p k n", p=P))
                load(1, up[:, bass.ds(at, 256)].rearrange("(k p) n -> p k n", p=P))
                load(2, down[bass.ds(at, 256), :].rearrange("(k p) n -> p k n", p=P))

            def ffn(gate, up, down, first=0):
                with n.loop(sp, STEPS - first, "step") as j:
                    ffn_step(gate, up, down, j * 256 + 256 * first)

            sp.dma_start(con[:, :], a["consts"]).then_inc(s["consts_in"], 16)
            sp.dma_start(XC[:, 0:8, :].rearrange("p (t k) n -> p t (k n)", t=2),
                         a["x"][0].rearrange("(t p) d -> p t d", p=P)).then_inc(s["x_in"], 16)
            with n.loop(sp, DEPTH, "layer") as l:
                ffn1 = a["ffn1_w_gate"][l], a["ffn1_w_up"][l], a["ffn1_w_down"][l]
                ffn_step(*ffn1, 0)
                sp.wait_ge(s["h_ready"], n.due("h_ready"))
                row = 0
                for name in ("ffn1_pre_g", "ffn1_post_g", "mix_pre_g", "mix_post_g", "ffn2_pre_g", "ffn2_post_g",
                             "ssd_norm_g", "s5_d", "ssd_conv_b"):
                    src = a[name][l].rearrange("(k p) -> k p", p=P)
                    sp.dma_start(prm_rows[row:row + src.shape[0], 0, :], src).then_inc(s["params_in"], 16)
                    row += src.shape[0]
                sp.dma_start(prm_rows[0:96, 1, :], a["ssd_conv_w"][l].rearrange("w (k p) -> (w k) p", p=P))\
                  .then_inc(s["params_in"], 16)
                for i, name in enumerate(("s5_lambda_re", "s5_lambda_im")):
                    sp.dma_start(s5_rows[:, i, :].rearrange("q (g n) -> q g n", g=2),
                                 a[name][l].rearrange("(q g) n -> q g n", g=2)).then_inc(s["params_in"], 16)
                sp.dma_start(s5_small[:, 0:2], a["s5_log_step"][l].rearrange("(q g) -> q g", g=2))\
                  .then_inc(s["params_in"], 16)
                sp.dma_start(s5_small[0:16, 2:4], a["ssd_d"][l].rearrange("(q g) -> q g", g=2))\
                  .then_inc(s["params_in"], 16)
                sp.dma_start(head_rows[:, 0:1], a["ssd_dt_bias"][l].rearrange("(h o) -> h o", o=1))\
                  .then_inc(s["params_in"], 16)
                sp.dma_start(head_rows[:, 1:2], a["ssd_a_log"][l].rearrange("(h o) -> h o", o=1))\
                  .then_inc(s["params_in"], 16)
                for i, part in enumerate(("re", "im")):
                    sp.dma_start(b_raw[:, i, :, :], a["s5_b_" + part][l].rearrange("(q g) n c -> (g n) q c", g=2))\
                      .then_inc(s["params_in"], 16)
                    sp.dma_start(c_raw[:, i, :, :], a["s5_c_" + part][l].rearrange("(t g) c n -> (g c) t n", g=8))\
                      .then_inc(s["params_in"], 16)
                ffn(*ffn1, first=1)
                c = MIX
                z0, xbc0, dt0, u0, ga0 = 0, INNER, INNER + 3072, INNER + 3072 + 32, INNER + 3072 + 32 + D
                cols = [u0 + 256 * i for i in range(4)] + [dt0] + [xbc0 + 256 * i for i in range(12)] \
                    + [ga0 + 256 * i for i in range(8)] + [z0 + 256 * i for i in range(8)]
                for col in cols:
                    w = P if col == dt0 else 256
                    load(c % RING, chunk_c(a["w_in"][l], col, w), 8 * w, alone=(col == 0))
                    c += 1
                for i in range(8):
                    load(c % RING, chunk_r(a["w_branch_a"][l], 256 * i))
                    c += 1
                for kind, i in GLU_ORDER:
                    src = chunk_r(a["w_branch_b"][l], 256 * i) if kind == "b" else \
                        chunk_c(a["s5_w_glu"][l], 256 * i + (D if kind == "g" else 0))
                    load(c % RING, src)
                    c += 1
                for i in range(4):
                    load(c % RING, chunk_r(a["w_out"][l], 256 * i))
                    c += 1
                assert c == FFN2
                ffn(a["ffn2_w_gate"][l], a["ffn2_w_up"][l], a["ffn2_w_down"][l])
                n.due("h_ready", 2)
            c = [0]

            def next_chunk(src):
                load(c[0] % RING, src)
                c[0] += 1

            def mem_chunks(l):
                for i in range(2):
                    next_chunk(chunk_c(a["w_mem_kv_2"][l], 256 * i))

            mem_chunks(0)
            next_chunk(chunk_c(a["w_mem_kv_2"][1], 0))
            sp.wait_ge(s["h_ready"], n.due("h_ready"))
            sp.dma_start(x_tok, a["mem_2"][0].rearrange("(t p) d -> p t d", p=P)).then_inc(s["mem_in"], 16)
            row = 0
            for name in ("ln1_g_2", "ln1_b_2", "ln2_g_2", "ln2_b_2", "conv_a_2"):
                src = a[name].rearrange("l (k p) -> (l k) p", p=P) if name != "conv_a_2" else \
                    a[name][0].rearrange("w (k p) -> (w k) p", p=P)
                sp.dma_start(prm_rows[row:row + src.shape[0], 0, :], src).then_inc(s["params2_in"], 16)
                row += src.shape[0]
            assert row == ROWS2
            sp.dma_start(positions.bitcast(I32), a["positions_2"][0:1, :].to_broadcast([P, T]))\
              .then_inc(s["params2_in"], 16)
            sp.dma_start(router, a["w_router_2"][0].rearrange("(k p) e -> p k e", p=P)).then_inc(s["params2_in"], 16)
            sp.dma_start(causal, a["causal"].rearrange("(t p) n -> p t n", p=P)).then_inc(s["params2_in"], 16)
            next_chunk(chunk_c(a["w_mem_kv_2"][1], 256))
            for i in range(10):
                next_chunk(chunk_c(a["w_in_a_2"][0], 256 * i))
            for i in range(4):
                next_chunk(chunk_r(a["w_o_2"][0], 256 * i))
            gu = a["w_gu_dense_2"][0]
            ffn(gu[:, 0:HID], gu[:, HID:2 * HID], a["w_down_dense_2"][0])
            c[0] += 3 * STEPS
            for i in range(6):
                next_chunk(chunk_c(a["w_kv_shared_2"], 256 * i))
            for i in range(4):
                next_chunk(chunk_c(a["w_q_b_2"][0], 256 * i))
            for i in range(4):
                next_chunk(chunk_r(a["w_o_2"][1], 256 * i))

            def expert_step(e, at):
                gu = a["w_gu_moe_2"][0][e]
                load(MOE_SLOTS[0], gu[:, bass.ds(at, 256)].rearrange("(k p) n -> p k n", p=P))
                load(MOE_SLOTS[1], gu[:, bass.ds(at + HID, 256)].rearrange("(k p) n -> p k n", p=P))
                load(MOE_SLOTS[2], a["w_down_moe_2"][0][e][bass.ds(at, 256), :].rearrange("(k p) n -> p k n", p=P))

            def expert_rest(e):
                with n.loop(sp, STEPS - 1, "moe_step") as j:
                    expert_step(e, j * 256 + 256)

            expert_step(0, 0)
            sp.wait_ge(s["routed"], n.due("routed"))
            passes = sp.value_load(n_pass[0:1, :].bitcast(I32), min_val=1, max_val=2)
            with n.loop(sp, passes, "pass"):
                with n.loop(sp, N_EXPERTS - 1, "expert") as e:
                    expert_rest(e)
                    expert_step(e + 1, 0)
                expert_rest(N_EXPERTS - 1)
                expert_step(0, 0)
            sp.wait_ge(s["out_ready"], n.due("out_ready"))
            sp.dma_start(out[0].rearrange("(t p) d -> p t d", p=P), x_tok).then_inc(s["out_sent"], 16)
            sp.wait_ge(s["out_sent"], n.due("out_sent", 16))

        @block.tensor
        def _(pe):
            n = Count()
            mm = nc.tensor.matmul
            run = [0, 0]


            def product(dst, slot, hi, lo, w0, start):
                mm(dst, w_hi[:, slot, w0:w0 + P], hi, start=start, stop=False, skip_group_check=True)
                mm(dst, w_lo[:, slot, w0:w0 + P], hi, start=False, stop=False, skip_group_check=True)
                return mm(dst, w_hi[:, slot, w0:w0 + P], lo, start=False, stop=True, skip_group_check=True)

            def col_tile(dst, slot, u, width=256, tokens=T):
                for k in range(DT):
                    last = product(dst, slot, x_hi[:, k, 0:tokens], x_lo[:, k, 0:tokens], k * width + u * P, k == 0)
                return last

            def c_chunk(c, tiles=2, width=256):
                if run[1] >= 2:
                    pe.wait_ge(s["c_evicted"], n.due("c_evicted"))
                bank = 4 + run[0] % 2
                run[0] += 1
                run[1] += 1
                pe.wait_ge(s["weights_ready"], n.due("weights_ready"))
                for u in range(tiles):
                    last = col_tile(PS[:, bank, u * T:(u + 1) * T], c % RING, u, width)
                last.then_inc(s["chunk_used"], n.one("chunk_used"))

            def end_run(waiting=False):
                v = n.due("c_evicted", min(2, run[1]))
                if waiting:
                    pe.wait_ge(s["c_evicted"], v)
                run[0] = run[1] = 0

            def r_tile(slot, kt, k):
                for o in range(DT):
                    last = product(ACC[:, o, :], slot, k_hi[:, k, :], k_lo[:, k, :], kt * D + o * P, False)
                return last

            def r_chunk(c, i):
                pe.wait_ge(s["weights_ready"], n.due("weights_ready"))
                for kt in range(2):
                    pe.wait_ge(s["staged"], n.due("staged"))
                    last = r_tile(c % RING, kt, (2 * i + kt) % 4)
                last.then_inc(s["chunk_used"], n.one("chunk_used"))

            def zero_acc():
                for b in range(4):
                    mm(PS[:, b, :], zero_bf[0:1, :], zero_bf[0:1, 0:1].to_broadcast([1, 512]), start=True, stop=True,
                       skip_group_check=True)

            def sum_features(src, bank, tiles=DT):
                for k in range(tiles):
                    last = mm(PS[:, bank, 0:T], cst("ones"), src[:, k, :], start=(k == 0), stop=(k == tiles - 1))
                return last

            def norm_sum():
                pe.wait_ge(s["squared"], n.due("squared"))
                sum_features(squares, 4).then_inc(s["summed"], n.one("summed"))

            def ffn():
                pe.wait_ge(s["x_ready"], n.due("x_ready", 2))
                zero_acc()
                with n.loop(pe, STEPS, "step"):
                    pe.wait_ge(s["weights_ready"], n.due("weights_ready"))
                    col_tile(PS[:, 4, 0:T], 0, 0).then_inc(s["gate_a"], n.one("gate_a"))
                    pe.wait_ge(s["weights_ready"], n.due("weights_ready"))
                    col_tile(PS[:, 5, 0:T], 1, 0).then_inc(s["up_a"], n.one("up_a"))
                    col_tile(PS[:, 6, 0:T], 0, 1).then_inc(s["chunk_used"], n.one("chunk_used"))
                    col_tile(PS[:, 7, 0:T], 1, 1).then_inc(s["chunk_used"], n.one("chunk_used"))
                    r_chunk(2, 0)

            def s5_step(k):
                if 1 <= k <= S5_PAIRS:
                    q, t = k - 1, (k - 1) // 4
                    if q % 4 == 0:
                        pe.wait_ge(s["mats_ready"], n.due("mats_ready"))
                    if q >= 2:
                        pe.wait_ge(s["modulated"], n.due("modulated"))
                    r = 32 * (q % 4)
                    for i in range(2):
                        last = mm(PS[:, 6 + q % 2, i * T:(i + 1) * T], mats[r:r + 32, i, :], U5[r:r + 32, t, :],
                                  start=(i == 0), stop=True, skip_group_check=True)
                    last.then_inc(s["bu_done"], n.one("bu_done"))
                if k % 4 == 0 and k < S5_PAIRS:
                    pe.wait_ge(s["mats_masked"], n.due("mats_masked"))
                    for i in range(4):
                        last = nc.tensor.transpose(PS[:, 0, i * P:(i + 1) * P], mats_in[:, i, :], cst("ident"))
                    last.then_inc(s["mats_psum"], n.one("mats_psum"))
                if k >= 3:
                    q = k - 3
                    if q % 4 == 0:
                        pe.wait_ge(s["cproj_ready"], n.due("cproj_ready"))
                        if q >= 8:
                            pe.wait_ge(s["y5_added"], n.due("y5_added"))
                    pe.wait_ge(s["h5_ready"], n.due("h5_ready"))
                    r = 32 * (q % 4)
                    for i in range(2):
                        last = mm(PS[r:r + 32, 1 + (q // 4) % 2, 0:T], cproj[:, (q // 4) % 2, i * P + r:i * P + r + 32],
                                  h5[:, i, :], start=(i == 0), stop=(i == 1), skip_group_check=True)
                    last.then_inc(s["y5_psum"], n.one("y5_psum"))

            def ssd_prepare(i):
                g = i // 2
                if i == 0:
                    pe.wait_ge(s["y5_added"], n.due("y5_added", 2))
                    pe.wait_ge(s["silu_conv"], n.due("silu_conv", 12))
                    pe.wait_ge(s["dtok_ready"], n.due("dtok_ready"))
                if i % 2 == 0:
                    if g:
                        pe.wait_ge(s["gm_ready"], n.due("gm_ready"))
                    mm(PS[:, 2, 0:T], XC[:, 16 + g, 0:P], XC[:, 20 + g, :], start=True, stop=True, skip_group_check=True)
                    mm(PS[:, 2, T:T + P], XC[:, 16 + g, P:T], XC[:, 20 + g, P:T], start=False, stop=True,
                       skip_group_check=True).then_inc(s["gm_psum"], n.one("gm_psum"))
                if i:
                    pe.wait_ge(s["decay_ready"], n.due("decay_ready", 4))
                for h in range(4):
                    last = mm(PS[:, h // 2, (h % 2) * T:(h % 2 + 1) * T],
                              cst("ident", 32, 4 * i + h, 1).to_broadcast([32, P]), dt_rows[:, 4, :],
                              start=(h % 2 == 0), stop=True, skip_group_check=True)
                    if h % 2:
                        last.then_inc(s["cum_psum"], n.one("cum_psum"))
                if i:
                    pe.wait_ge(s["xt_ready"], n.due("xt_ready"))
                for t in range(2):
                    for u in range(2):
                        last = nc.tensor.transpose(PS[:, 3, (2 * t + u) * P:(2 * t + u + 1) * P],
                                                   XC[:, 2 * i + u, t * P:(t + 1) * P], cst("ident"))
                last.then_inc(s["xt_psum"], n.one("xt_psum"))

            def ssd_output(i):
                if i == 7:
                    pe.wait_ge(s["xt_ready"], n.due("xt_ready"))
                for u in range(2):
                    if i >= 1:
                        pe.wait_ge(s["y_ready"], n.due("y_ready"))
                    for hh in range(2):
                        pe.wait_ge(s["masked"], n.due("masked"))
                        o, w = 64 * hh, xt[:, i % 2, :]
                        d = decay[:, i % 2, 2 * u + hh, :]
                        mm(PS[o:o + 64, 6 + u, 0:T], w[:, u * P + o:u * P + o + 64], d[:, 0:T],
                           start=True, stop=True, skip_group_check=True)
                        last = mm(PS[o:o + 64, 6 + u, P:T], w[:, T + u * P + o:T + u * P + o + 64], d[:, T:T + P],
                                  start=False, stop=True, skip_group_check=True)
                    last.then_inc(s["y_psum"], n.one("y_psum"))

            def turn_row(dst, src):
                return mm(dst, src, cst("ident", 32, 0, 32), start=True, stop=True, skip_group_check=True)

            def mixer():
                pe.wait_ge(s["x_ready"], n.due("x_ready", 2))
                for k, (kind, i) in enumerate(TICKS):
                    c_chunk(MIX + k, *((1, P) if kind == "d" else ()))
                    if k == 3:
                        pe.wait_ge(s["s5_ready"], n.due("s5_ready"))
                        for j in range(6):
                            turn_row(PS[:, 7, 32 * j:32 * j + 32], s5row[:, j, :])
                        nc.tensor.transpose(PS[:, 7, 192:208], s5row[0:16, 6, :], cst("ident", 16, 0, 16))\
                          .then_inc(s["s5_psum"], n.one("s5_psum"))
                    for q in S5_AT[k]:
                        s5_step(q)
                    if kind == "g" and i == 7:
                        n.due("modulated", 2)
                        pe.wait_ge(s["dt_rows_ready"], n.due("dt_rows_ready"))
                        for j, (row, lo) in enumerate(((3, 0), (3, P), (4, 0), (4, P), (1, 0))):
                            last = turn_row(PS[:, 3, 32 * j:32 * j + 32], dt_rows[:, row, lo:lo + P])
                        last.then_inc(s["dtok_psum"], n.one("dtok_psum"))
                    if kind == "z":
                        ssd_prepare(i)
                        if i:
                            ssd_output(i - 1)
                ssd_output(7)
                end_run()
                n.due("gm_ready")
                n.due("decay_ready", 4)
                for g in range(GROUPS):
                    if g == 2:
                        pe.wait_ge(s["y_ready"], n.due("y_ready", 2))
                    pe.wait_ge(s["group_sq"], n.due("group_sq"))
                    sum_features(group_squares[g % 2], 4 + g, 4).then_inc(s["group_sum"], n.one("group_sum"))
                zero_acc()
                for i in range(8):
                    r_chunk(C_A + i, i)
                pe.wait_ge(s["x_ready"], n.due("x_ready", 2))
                for k, (kind, i) in enumerate(GLU_ORDER):
                    if (kind, i) == ("b", 0):
                        pe.wait_ge(s["acc_read"], n.due("acc_read"))
                        zero_acc()
                    if kind == "b":
                        r_chunk(C_G + k, i)
                    else:
                        c_chunk(C_G + k)
                end_run()
                pe.wait_ge(s["acc_read"], n.due("acc_read"))
                zero_acc()
                for i in range(4):
                    r_chunk(C_OUT + i, i)

            pe.sem_inc(s["chunk_used"], RING)
            n.given["chunk_used"] += RING
            n.due("weights_ready", RING)
            pe.wait_ge(s["consts_in"], 16)
            pe.wait_ge(s["x_in"], 16)
            pe.wait_ge(s["setup_done"], n.due("setup_done"))
            for k in range(DT):
                for t in range(2):
                    last = nc.tensor.transpose(ACC[:, k, t * P:(t + 1) * P], x_tok[:, t, k * P:(k + 1) * P], cst("ident"))
            last.then_inc(s["x_turned"], n.one("x_turned"))
            with n.loop(pe, DEPTH, "layer"):
                pe.wait_ge(s["params_in"], n.due("params_in", 16 * 20))
                for i in range(2):
                    last = nc.tensor.transpose(PS[:, 7, 96 * i:96 * i + 96], prm_rows[0:96, i, :], cst("ident", 96, 0, 96))
                last.then_inc(s["prm_psum"], n.one("prm_psum"))
                norm_sum()
                pe.wait_ge(s["prm_ready"], n.due("prm_ready"))
                ffn()
                norm_sum()
                norm_sum()
                mixer()
                norm_sum()
                norm_sum()
                ffn()
                norm_sum()

            def row_tile(dst, slot, t):
                for k in range(DT):
                    hi, lo = (x[:, k, t * P:(t + 1) * P] for x in (x_hi, x_lo))
                    whi, wlo = (x[:, slot, k * 256:(k + 1) * 256] for x in (w_hi, w_lo))
                    mm(dst, hi, whi, start=(k == 0), stop=False, skip_group_check=True)
                    mm(dst, lo, whi, start=False, stop=False, skip_group_check=True)
                    last = mm(dst, hi, wlo, start=False, stop=True, skip_group_check=True)
                return last

            def v_chunk(c):
                if run[1] >= 2:
                    pe.wait_ge(s["c_evicted"], n.due("c_evicted"))
                bank = 4 + run[0] % 2
                run[0] += 1
                run[1] += 1
                pe.wait_ge(s["weights_ready"], n.due("weights_ready"))
                for t in range(2):
                    last = row_tile(PS[:, bank, t * T:(t + 1) * T], c % RING, t)
                last.then_inc(s["chunk_used"], n.one("chunk_used"))

            def turn_tokens(src, event):
                for k in range(DT):
                    for t in range(2):
                        last = nc.tensor.transpose(ACC[:, k, t * P:(t + 1) * P], src[:, t, k * P:(k + 1) * P], cst("ident"))
                last.then_inc(s[event], n.one(event))

            def turn_features(event):
                for t in range(2):
                    for k in range(DT):
                        last = nc.tensor.transpose(ACC_FLAT[:, t * D + k * P:t * D + (k + 1) * P],
                                                   H[:, k, t * P:(t + 1) * P], cst("ident"))
                last.then_inc(s[event], n.one(event))

            def attention(heads):
                for i in range(len(heads) + 2):
                    if i < len(heads):
                        q, k, _, _, _, _ = heads[i]
                        o = 64 * (i % 2)
                        for t in range(2):
                            last = mm(PS[:, i % 2, t * T:(t + 1) * T], q[o:o + 64, t * P:(t + 1) * P], k[o:o + 64, :],
                                      start=(t == 0), stop=True, skip_group_check=True)
                        last.then_inc(s["att_scores"], n.one("att_scores"))
                    if 1 <= i <= len(heads):
                        h = i - 1
                        pe.wait_ge(s["att_norm"], n.due("att_norm"))
                        for kt in range(2):
                            for t in range(2):
                                last = nc.tensor.transpose(PS[:, 2 + h % 2, kt * T + t * P:kt * T + (t + 1) * P],
                                                           probs[:, h % 2, t, kt * P:(kt + 1) * P], cst("ident"))
                        last.then_inc(s["att_turned"], n.one("att_turned"))
                    if i >= 2:
                        h = i - 2
                        _, _, vals, col, _, _ = heads[h]
                        o = 64 * (h % 2)
                        pe.wait_ge(s["att_copied"], n.due("att_copied"))
                        if h % 2 == 0 and h >= 4:
                            pe.wait_ge(s["att_evicted"], n.due("att_evicted"))
                        for kt in range(2):
                            last = mm(PS[o:o + 64, 6 + (h // 2) % 2, 0:T], vals[:, kt, col:col + 64], probs_t[:, h % 2, kt, :],
                                      start=(kt == 0), stop=(kt == 1), skip_group_check=True)
                        if h % 2:
                            last.then_inc(s["att_out"], n.one("att_out"))
                n.due("att_evicted", min(2, len(heads) // 2))

            def layer_norm():
                pe.wait_ge(s["h_ready"], n.due("h_ready"))
                sum_features(H, 4).then_inc(s["mean_sum"], n.one("mean_sum"))
                norm_sum()

            pe.wait_ge(s["params2_in"], n.due("params2_in", 16 * 8))
            nc.tensor.transpose(PS[:, 7, 0:ROWS2], prm_rows[0:ROWS2, 0, :], cst("ident", ROWS2, 0, ROWS2))\
              .then_inc(s["prm_psum"], n.one("prm_psum"))
            pe.wait_ge(s["mem_in"], n.due("mem_in", 16))
            pe.wait_ge(s["h_ready"], n.due("h_ready", 1 + 3 * DEPTH))
            turn_tokens(x_tok, "x_turned")
            pe.wait_ge(s["x_ready"], n.due("x_ready", 2))
            pe.wait_ge(s["prm_ready"], n.due("prm_ready"))
            for l in range(2):
                c_chunk(B_MEM + 2 * l)
                v_chunk(B_MEM + 2 * l + 1)
            pe.wait_ge(s["x_ready"], n.due("x_ready", 2))
            for i in range(10):
                c_chunk(B_INA + i)
            end_run(waiting=True)
            attention(heads_a)
            zero_acc()
            for i in range(4):
                r_chunk(B_WO1 + i, i)
            layer_norm()
            ffn()
            layer_norm()
            pe.wait_ge(s["x_ready"], n.due("x_ready", 2))
            for i in range(3):
                c_chunk(B_KV + i)
            for i in range(3):
                v_chunk(B_KV + 3 + i)
            for i in range(4):
                c_chunk(B_Q + i)
            end_run(waiting=True)
            for i, t in enumerate(rope_tiles):
                if i >= 2:
                    pe.wait_ge(s["roped"], n.due("roped"))
                mm(PS[:, 6 + i % 2, 0:T], cst("swap"), XC[:, t, :], start=True, stop=True)\
                  .then_inc(s["rope_psum"], n.one("rope_psum"))
            pe.wait_ge(s["roped"], n.due("roped", 2))
            attention(heads_b)
            zero_acc()
            for i in range(4):
                r_chunk(B_WO2 + i, i)
            layer_norm()
            pe.wait_ge(s["normed"], n.due("normed"))
            for t in range(2):
                for k in range(DT):
                    last = mm(PS[:, 4, 8 * t:8 * t + 8], H[:, k, t * P:(t + 1) * P], router[:, k, :],
                              start=(t == 0 and k == 0), stop=(k == DT - 1), skip_group_check=True)
            last.then_inc(s["logits"], n.one("logits"))
            turn_features("tokens_turned")
            pe.wait_ge(s["masks_ready"], n.due("masks_ready"))
            for t in range(2):
                mm(PS[:, 5, 8 * t:8 * t + 8], cst("before"), chosen[:, t, :], start=(t == 0), stop=True,
                   skip_group_check=True)
            mm(PS[:, 5, 8:16], cst("ones"), chosen[:, 0, :], start=False, stop=True, skip_group_check=True)
            for t in range(2):
                last = mm(PS[:, 5, 16:24], cst("ones"), chosen[:, t, :], start=False, stop=True, skip_group_check=True)
            last.then_inc(s["ranks"], n.one("ranks"))
            pe.wait_ge(s["routed"], n.due("routed"))
            passes = pe.value_load(n_pass[0:1, :].bitcast(I32), min_val=1, max_val=2)

            def gather():
                pe.wait_ge(s["picked"], n.due("picked"))
                for k in range(DT):
                    for t in range(2):
                        last = mm(PS[:, 2 + k // 4, (k % 4) * P:(k % 4 + 1) * P], x_tok[:, t, k * P:(k + 1) * P],
                                  pick[:, t, :], start=(k % 4 == 0 and t == 0), stop=(t == 1), skip_group_check=True)
                last.then_inc(s["gathered"], n.one("gathered"))

            def turn_scatter():
                for t in range(2):
                    last = nc.tensor.transpose(PS[:, 4, t * P:(t + 1) * P], pick[:, 2 + t, :], cst("ident"))
                last.then_inc(s["scatter_turned"], n.one("scatter_turned"))

            pe.wait_ge(s["tokens_ready"], n.due("tokens_ready"))
            gather()
            turn_scatter()
            pe.wait_ge(s["scatter_ready"], n.due("scatter_ready"))
            pe.wait_ge(s["x_ready"], n.due("x_ready", 2))
            with n.loop(pe, passes, "pass"):
                with n.loop(pe, N_EXPERTS, "expert"):
                    pe.wait_ge(s["sum_added"], n.due("sum_added"))
                    for b in range(2):
                        mm(PS[:, b, :], zero_bf[0:1, :], zero_bf[0:1, 0:1].to_broadcast([1, 512]), start=True, stop=True,
                           skip_group_check=True)
                    g_, u_, d_ = MOE_SLOTS
                    with n.loop(pe, STEPS, "moe_step"):
                        for bank, slot in ((4, g_), (5, u_)):
                            pe.wait_ge(s["weights_ready"], n.due("weights_ready"))
                            row_tile(PS[:, bank, 0:T], slot, 0).then_inc(s["chunk_used"], n.one("chunk_used"))
                        pe.wait_ge(s["hidden_ready"], n.due("hidden_ready"))
                        for kt in range(2):
                            last = nc.tensor.transpose(PS[:, 6, kt * P:(kt + 1) * P], stage[:, 0, kt * P:(kt + 1) * P],
                                                       cst("ident"))
                        last.then_inc(s["hidden_turned"], n.one("hidden_turned"))
                        pe.wait_ge(s["weights_ready"], n.due("weights_ready"))
                        pe.wait_ge(s["staged"], n.due("staged"))
                        for kt in range(2):
                            hi, lo = k_hi[:, kt, 0:P], k_lo[:, kt, 0:P]
                            for b in range(2):
                                whi, wlo = (w[:, d_, kt * D + 512 * b:kt * D + 512 * (b + 1)] for w in (w_hi, w_lo))
                                mm(PS[:, b, :], hi, whi, start=False, stop=True, skip_group_check=True)
                                mm(PS[:, b, :], lo, whi, start=False, stop=True, skip_group_check=True)
                                last = mm(PS[:, b, :], hi, wlo, start=False, stop=True, skip_group_check=True)
                        last.then_inc(s["chunk_used"], n.one("chunk_used"))
                    pe.wait_ge(s["sum_added"], n.due("sum_added"))
                    gather()
                    pe.wait_ge(s["y_copied"], n.due("y_copied"))
                    for k in range(DT):
                        if k == 4:
                            pe.wait_ge(s["x_ready"], n.due("x_ready", 2))
                        last = mm(PS[:, (6, 7, 2, 3)[k // 2], (k % 2) * T:(k % 2 + 1) * T], y_exp[:, k * P:(k + 1) * P],
                                  scatter, start=(k % 2 == 0), stop=True, skip_group_check=True)
                        if k % 4 == 3:
                            last.then_inc(s["scattered"], n.one("scattered"))
                    turn_scatter()
                    pe.wait_ge(s["scatter_ready"], n.due("scatter_ready"))
            layer_norm()
            pe.wait_ge(s["normed"], n.due("normed"))
            turn_features("out_turned")

        @block.scalar
        def _(act):
            n = Count()
            fn = nc.scalar.activation
            pos = [-1]
            run = [0]


            def convert(slot):
                act.wait_ge(s[LANDED[slot]], n.due(LANDED[slot], 16))
                act.wait_ge(s["chunk_used"], n.due("chunk_used"))
                pos[0] += 1
                fn(w_hi[:, slot, :], raw[:, slot, :], ACT.Copy).then_inc(s["hi_ready"], n.one("hi_ready"))

            def wait_used(c):
                act.wait_ge(s["chunk_used"], n.peek("chunk_used", c - pos[0]))

            def root(width, eps=eps[:, 0:1]):
                act.wait_ge(s["summed"], n.due("summed"))
                fn(rstd[:, :], PS[:, 4, 0:T], ACT.Sqrt, bias=eps, scale=1.0 / width)\
                    .then_inc(s["rooted"], n.one("rooted"))

            def pre_norm(params=False):
                act.wait_ge(s["h_ready"], n.due("h_ready"))
                fn(squares, H[:, :, :], ACT.Square).then_inc(s["squared"], n.one("squared"))
                if params:
                    act.wait_ge(s["prm_psum"], n.due("prm_psum"))
                    fn(prm[:, :], PS[:, 7, 0:192], ACT.Copy).then_inc(s["prm_ready"], n.one("prm_ready"))
                root(D)
                for i in range(2):
                    act.wait_ge(s["xf_ready"], n.due("xf_ready"))
                    fn(x_hi[:, 4 * i:4 * i + 4, :], squares[:, 4 * i:4 * i + 4, :], ACT.Copy)\
                        .then_inc(s["xh_ready"], n.one("xh_ready"))

            def post_norm():
                fn(squares.rearrange("p k n -> p (k n)"), ACC_FLAT, ACT.Square).then_inc(s["squared"], n.one("squared"))
                root(D)

            def ffn():
                with n.loop(act, STEPS, "step"):
                    act.wait_ge(s["gate_a"], n.due("gate_a"))
                    fn(act_out[:, 0, :], PS[:, 4, 0:T], ACT.Silu).then_inc(s["silu_done"], n.one("silu_done"))
                    wait_used(pos[0] + 1)
                    fn(act_out[:, 1, :], PS[:, 6, 0:T], ACT.Silu).then_inc(s["silu_done"], n.one("silu_done"))
                    for slot in range(RING):
                        convert(slot)
                    n.due("staged", 2)
                pos[0] += RING * (STEPS - 1)

            def evict(dst, func):
                wait_used(pos[0] + 1)
                fn(dst, PS[:, 4 + run[0] % 2, :].rearrange("p (u n) -> p u n", u=2), func)\
                    .then_inc(s["c_evicted"], n.one("c_evicted"))
                run[0] += 1

            def s5_step(k):
                if k < S5_PAIRS:
                    m = k % 3
                    if k >= 3:
                        act.wait_ge(s["g_ready"], n.due("g_ready"))
                    act.wait_ge(s["turns_ready"], n.due("turns_ready"))
                    fn(sin_t[:, m, :], turns[:, 0, :], ACT.Sin, scale=2 * PI_BELOW)
                    fn(turns[:, 1, :], turns[:, 0, :], ACT.Abs).then_inc(s["act_step"], n.one("act_step"))
                    act.wait_ge(s["act_step"], n.last("act_step"))
                    fn(cos_t[:, m, :], turns[:, 1, :], ACT.Sin, scale=-2 * PI_BELOW, bias=eps[:, 1:2])\
                        .then_inc(s["table_ready"], n.one("table_ready"))
                if k % 4 == 0 and k < S5_PAIRS:
                    if k:
                        act.wait_ge(s["cproj_ready"], n.due("cproj_ready"))
                    act.wait_ge(s["mats_psum"], n.due("mats_psum"))
                    fn(mats.rearrange("p a n -> p (a n)"), PS[:, 0, :], ACT.Copy)\
                        .then_inc(s["mats_ready"], n.one("mats_ready"))
                if k % 4 == 0 and k >= 8:
                    gelu(k // 4 - 2)

            def gelu(t):
                act.wait_ge(s["y5_added"], n.due("y5_added"))
                fn(U5[:, t, :], U5[:, t, :], ACT.Gelu_apprx_tanh).then_inc(s["y5_done"], n.one("y5_done"))

            def silu_conv(i):
                act.wait_ge(s["tap_done"], n.due("tap_done"))
                fn(XC[:, 2 * i:2 * i + 2, :], conv_out[:, i % 2, :, :], ACT.Silu)\
                    .then_inc(s["silu_conv"], n.one("silu_conv"))

            def ssd_decay(i):
                if i == 0:
                    act.wait_ge(s["dtok_ready"], n.due("dtok_ready"))
                if i >= 2:
                    act.wait_ge(s["y_psum"], n.due("y_psum", 2))
                for h in range(4):
                    hd, d = 4 * i + h, decay[:, i % 2, h, :]
                    if h % 2 == 0:
                        act.wait_ge(s["cum_psum"], n.due("cum_psum"))
                    row = PS[:, h // 2, (h % 2) * T:(h % 2 + 1) * T]
                    fn(d[:, P:T], row[:, P:T], ACT.Exp, bias=dt_tok[:, 4, hd:hd + 1])
                    fn(d[:, 0:P], row[:, 0:P], ACT.Relu, scale=-1.0, bias=dt_tok[:, 2, hd:hd + 1])
                    fn(d[:, T:T + P], row[:, P:T], ACT.Relu, scale=-1.0, bias=dt_tok[:, 3, hd:hd + 1])\
                        .then_inc(s["act_step"], n.one("act_step"))
                    act.wait_ge(s["act_step"], n.last("act_step"))
                    dd = d.rearrange("p (a n) -> p a n", n=P)[:, 0:3:2, :]
                    fn(dd, dd, ACT.Exp, scale=-1.0).then_inc(s["decay_ready"], n.one("decay_ready"))

            def group_root(g):
                act.wait_ge(s["group_sum"], n.due("group_sum"))
                fn(group_rstd[:, g, :], PS[:, 4 + g, 0:T], ACT.Sqrt, bias=eps[:, 0:1], scale=GROUPS / INNER)\
                    .then_inc(s["group_root"], n.one("group_root"))

            def mixer():
                run[0] = 0
                for k, (kind, i) in enumerate(TICKS):
                    if k == 1:
                        act.wait_ge(s["s5_step"], n.due("s5_step"))
                        fn(s5row[:, 7, :], s5row[:, 7, :], ACT.Exp)
                        fn(head_rows[:, 1:2], head_rows[:, 1:2], ACT.Exp).then_inc(s["s5_exp"], n.one("s5_exp"))
                    if k == 2:
                        act.wait_ge(s["s5_step"], n.due("s5_step"))
                        fn(s5row[:, 9, :], s5row[:, 8, :], ACT.Sin)
                        fn(s5row[:, 10, :], s5row[:, 8, :], ACT.Abs).then_inc(s["act_step"], n.one("act_step"))
                        act.wait_ge(s["act_step"], n.last("act_step"))
                        fn(s5row[:, 10, :], s5row[:, 10, :], ACT.Sin, scale=-1.0, bias=eps[0:32, 1:2])\
                            .then_inc(s["s5_exp"], n.one("s5_exp"))
                    if k == 6:
                        act.wait_ge(s["dt_step"], n.due("dt_step"))
                        fn(dt_rows[:, 1, :], dt_rows[:, 1, :], ACT.Exp).then_inc(s["dt_act"], n.one("dt_act"))
                        act.wait_ge(s["dt_step"], n.due("dt_step"))
                        fn(dt_rows[:, 3, :], dt_rows[:, 2, :], ACT.Ln).then_inc(s["dt_act"], n.one("dt_act"))
                    for q in S5_AT[k]:
                        s5_step(q)
                    if 7 <= k < 19:
                        silu_conv(k - 7)
                    if k == 25:
                        gelu(7)
                    if kind == "z" and i:
                        ssd_decay(i - 1)
                    if kind == "z" and i >= 3:
                        act.wait_ge(s["y_ready"], n.due("y_ready", 2))
                    if kind == "u":
                        evict(U5[:, 2 * i:2 * i + 2, :], ACT.Copy)
                    if kind == "d":
                        wait_used(pos[0] + 1)
                        fn(dt_rows[:, 0, :], PS[0:32, 4 + run[0] % 2, 0:T], ACT.Identity, bias=head_rows[:, 0:1])\
                            .then_inc(s["c_evicted"], n.one("c_evicted"))
                        run[0] += 1
                    if kind == "x":
                        evict(conv_in[:, i % 2, :, 3:T + 3], ACT.Copy)
                    if kind == "g":
                        if i == 4:
                            pass
                        evict(G[:, 2 * i:2 * i + 2, :], ACT.Sigmoid)
                    if kind == "z":
                        evict(zbuf[i % 3], ACT.Silu)
                    convert((MIX + k) % RING)
                ssd_decay(7)
                n.due("y_psum", 4)
                n.due("g_ready", 3)
                n.due("cproj_ready")
                for g in range(GROUPS):
                    if g >= 2:
                        act.wait_ge(s["y_ready"], n.due("y_ready", 2 * g - 2))
                        group_root(g - 2)
                    fn(group_squares[g % 2], XC[:, 4 * g:4 * g + 4, :], ACT.Square)\
                        .then_inc(s["group_sq"], n.one("group_sq"))
                for g in (2, 3):
                    group_root(g)
                act.wait_ge(s["y5_done"], n.last("y5_done"))
                for i in range(2):
                    fn(x_hi[:, 4 * i:4 * i + 4, :], U5[:, 4 * i:4 * i + 4, :], ACT.Copy)\
                        .then_inc(s["xh_ready"], n.one("xh_ready"))
                for i in range(8):
                    convert((C_A + i) % RING)
                n.due("staged", 16)
                run[0] = 0
                for k, (kind, i) in enumerate(GLU_ORDER):
                    if kind == "v":
                        if i >= 2:
                            act.wait_ge(s["staged"], n.due("staged", 2))
                        evict(conv_out[:, i % 2], ACT.Copy)
                    if kind == "g":
                        evict(glu_gate[:, i % 2], ACT.Sigmoid)
                    convert((C_G + k) % RING)
                n.due("staged", 4)
                for i in range(4):
                    convert((C_OUT + i) % RING)
                n.due("staged", 8)

            act.wait_ge(s["setup_done"], n.due("setup_done"))
            for slot in range(RING):
                convert(slot)
            with n.loop(act, DEPTH, "layer"):
                pos[0] = -1
                pre_norm(params=True)
                ffn()
                post_norm()
                pre_norm()
                mixer()
                post_norm()
                pre_norm()
                ffn()
                post_norm()

            pos[0] = -1
            run[0] = 0

            def split_high(src):
                for i in range(2):
                    act.wait_ge(s["xf_ready"], n.due("xf_ready"))
                    fn(x_hi[:, 4 * i:4 * i + 4, :], src[:, 4 * i:4 * i + 4, :], ACT.Copy)\
                        .then_inc(s["xh_ready"], n.one("xh_ready"))

            def layer_norm(split=True):
                act.wait_ge(s["centered"], n.due("centered"))
                fn(squares, H[:, :, :], ACT.Square).then_inc(s["squared"], n.one("squared"))
                root(D, eps=eps[:, 2:3])
                if split:
                    split_high(H)

            def attention(heads):
                for i in range(len(heads) + 2):
                    if i < len(heads):
                        b, masked = i % 2, heads[i][5]
                        act.wait_ge(s["att_max"], n.due("att_max"))
                        for t in range(2):
                            src = probs[:, b, t, :] if masked else PS[:, b, t * T:(t + 1) * T]
                            last = fn(probs[:, b, t, :], src, ACT.Exp, scale=ATTN_SCALE, bias=att_small[:, b, 2 + t:3 + t],
                                      accum_out=att_small[:, b, 4 + t:5 + t])
                        last.then_inc(s["att_exp"], n.one("att_exp"))
                    if 1 <= i <= len(heads):
                        h = i - 1
                        act.wait_ge(s["att_turned"], n.due("att_turned"))
                        fn(probs_t[:, h % 2, :, :].rearrange("p k n -> p (k n)"), PS[:, 2 + h % 2, :], ACT.Copy)\
                            .then_inc(s["att_copied"], n.one("att_copied"))
                    if i >= 2 and i % 2:
                        act.wait_ge(s["att_out"], n.due("att_out"))
                        fn(heads[i - 2][4], PS[:, 6 + ((i - 2) // 2) % 2, 0:T], ACT.Copy)\
                            .then_inc(s["att_evicted"], n.one("att_evicted"))

            def r_chunks(c0):
                for i in range(4):
                    convert((c0 + i) % RING)

            act.wait_ge(s["prm_psum"], n.due("prm_psum"))
            fn(prm[:, 0:ROWS2], PS[:, 7, 0:ROWS2], ACT.Copy).then_inc(s["prm_ready"], n.one("prm_ready"))
            split_high(squares)
            act.wait_ge(s["rope_ang"], n.due("rope_ang"))
            fn(rope_sin, rope_a, ACT.Sin)
            fn(rope_b, rope_a, ACT.Abs).then_inc(s["act_step"], n.one("act_step"))
            act.wait_ge(s["act_step"], n.last("act_step"))
            fn(rope_cos, rope_b, ACT.Sin, scale=-1.0, bias=eps[:, 1:2]).then_inc(s["rope_table"], n.one("rope_table"))
            for l in range(2):
                for i in range(2):
                    evict(G[:, 4 * i + 2 * l:4 * i + 2 * l + 2, :], ACT.Copy)
                    if l == 1 and i == 1:
                        for j in range(2):
                            fn(x_hi[:, 4 * j:4 * j + 4, :], H[:, 4 * j:4 * j + 4, :], ACT.Copy)\
                                .then_inc(s["xh_ready"], n.one("xh_ready"))
                    convert((B_MEM + 2 * l + i) % RING)
            for i in range(10):
                evict(XC[:, 2 * i:2 * i + 2, :], ACT.Copy)
                convert((B_INA + i) % RING)
            attention(heads_a)
            r_chunks(B_WO1)
            layer_norm()
            ffn()
            layer_norm()
            run[0] = 0
            for i in range(3):
                evict(XC[:, 8 + 2 * i:10 + 2 * i, :], ACT.Copy)
                convert((B_KV + i) % RING)
            for i in range(3):
                evict(v_all[:, :, 256 * i:256 * (i + 1)], ACT.Copy)
                convert((B_KV + 3 + i) % RING)
            for i in range(4):
                evict(XC[:, 2 * i:2 * i + 2, :], ACT.Copy)
                convert((B_Q + i) % RING)
            attention(heads_b)
            r_chunks(B_WO2)
            layer_norm(split=False)
            act.wait_ge(s["tokens_turned"], n.due("tokens_turned"))
            fn(x_tok, ACC_FLAT.rearrange("p (t d) -> p t d", t=2), ACT.Copy).then_inc(s["tokens_ready"], n.one("tokens_ready"))
            act.wait_ge(s["gate_diff"], n.due("gate_diff"))
            fn(rsm[:, 5, :], rsm[:, 4, :], ACT.Exp).then_inc(s["route_exp"], n.one("route_exp"))
            act.wait_ge(s["routed"], n.due("routed"))
            passes = act.value_load(n_pass[0:1, :].bitcast(I32), min_val=1, max_val=2)

            def expert_inputs():
                act.wait_ge(s["gathered"], n.due("gathered"))
                for i in range(2):
                    fn(x_hi[:, 4 * i:4 * i + 4, 0:P], PS[:, 2 + i, :].rearrange("p (k n) -> p k n", n=P), ACT.Copy)\
                        .then_inc(s["xh_ready"], n.one("xh_ready"))
                act.wait_ge(s["scatter_turned"], n.due("scatter_turned"))
                fn(scatter, PS[:, 4, 0:T], ACT.Copy).then_inc(s["scatter_ready"], n.one("scatter_ready"))

            expert_inputs()
            with n.loop(act, passes, "pass"):
                with n.loop(act, N_EXPERTS, "expert"):
                    with n.loop(act, STEPS, "moe_step"):
                        wait_used(pos[0] + 1)
                        fn(act_out[:, 0, :], PS[:, 4, 0:T], ACT.Silu).then_inc(s["silu_done"], n.one("silu_done"))
                        convert(MOE_SLOTS[0])
                        act.wait_ge(s["hidden_turned"], n.due("hidden_turned"))
                        fn(k_hi[:, 0:2, 0:P], PS[:, 6, 0:T].rearrange("p (k n) -> p k n", n=P), ACT.Copy)                            .then_inc(s["kh_ready"], n.one("kh_ready"))
                        convert(MOE_SLOTS[1])
                        convert(MOE_SLOTS[2])
                    fn(y_exp, PS[:, 0:2, :].rearrange("p b n -> p (b n)"), ACT.Copy).then_inc(s["y_copied"], n.one("y_copied"))
                    expert_inputs()
            layer_norm(split=False)
            act.wait_ge(s["out_turned"], n.due("out_turned"))
            fn(x_tok, ACC_FLAT.rearrange("p (t d) -> p t d", t=2), ACT.Copy).then_inc(s["out_ready"], n.one("out_ready"))

        @block.vector
        def _(dve):
            n = Count()
            v = nc.vector
            tt, ts, stt = v.tensor_tensor, v.tensor_scalar, v.scalar_tensor_tensor
            pos = [-1]


            def then(ins):
                ins.then_inc(s["dve_step"], n.one("dve_step"))
                dve.wait_ge(s["dve_step"], n.last("dve_step"))

            def convert(slot):
                dve.wait_ge(s["hi_ready"], n.due("hi_ready"))
                tt(w_lo[:, slot, :], raw[:, slot, :], w_hi[:, slot, :].bitcast(F32), SUB)\
                    .then_inc(s["weights_ready"], n.one("weights_ready"))
                n.due("chunk_used")
                pos[0] += 1

            def wait_used(c):
                dve.wait_ge(s["chunk_used"], n.peek("chunk_used", c - pos[0]))

            def low_parts(src):
                for i in range(2):
                    dve.wait_ge(s["xh_ready"], n.due("xh_ready"))
                    tt(x_lo[:, 4 * i:4 * i + 4, :], src[:, 4 * i:4 * i + 4, :], x_hi[:, 4 * i:4 * i + 4, :].bitcast(F32), SUB)\
                        .then_inc(s["x_ready"], n.one("x_ready"))

            def pre_norm(g0):
                if g0 == 0:
                    dve.wait_ge(s["prm_ready"], n.due("prm_ready"))
                dve.wait_ge(s["rooted"], n.due("rooted"))
                then(v.reciprocal(rstd[:, :], rstd[:, :]))
                for k in range(DT):
                    ins = stt(squares[:, k, :], H[:, k, :], prm[:, g0 + k:g0 + k + 1], rstd[:, :], MULT, MULT)
                    if k % 4 == 3:
                        ins.then_inc(s["xf_ready"], n.one("xf_ready"))
                low_parts(squares)

            def post_norm(g0, factor):
                dve.wait_ge(s["rooted"], n.due("rooted"))
                then(v.reciprocal(rstd[:, :], rstd[:, :]))
                for k in range(DT):
                    ins = stt(squares[:, k, :], ACC[:, k, :], prm[:, g0 + k:g0 + k + 1], rstd[:, :], MULT, MULT)
                then(ins)
                flat = H[:, :, :].rearrange("p k n -> p (k n)")
                stt(flat, squares.rearrange("p k n -> p (k n)"), factor, flat, MULT, ADD)\
                    .then_inc(s["h_ready"], n.one("h_ready"))

            def stage_k(k, make, tokens=T):
                make(k_hi[:, k, 0:tokens])
                then(make(stage[:, k % 2, 0:tokens]))
                tt(k_lo[:, k, 0:tokens], stage[:, k % 2, 0:tokens], k_hi[:, k, 0:tokens].bitcast(F32), SUB)\
                    .then_inc(s["staged"], n.one("staged"))

            def ffn():
                with n.loop(dve, STEPS, "step"):
                    for u in range(2):
                        dve.wait_ge(s["silu_done"], n.due("silu_done"))
                        if u == 0:
                            dve.wait_ge(s["up_a"], n.due("up_a"))
                        else:
                            wait_used(pos[0] + 2)
                        stage_k(u, lambda dst: tt(dst, act_out[:, u, :], PS[:, 5 + 2 * u, 0:T], MULT))
                    for slot in range(RING):
                        convert(slot)
                pos[0] += RING * (STEPS - 1)

            def row(i):
                return s5row[:, i, :]

            def s5_rows_a():
                dve.wait_ge(s["x_ready"], n.last("x_ready"))
                v.tensor_copy(row(7).rearrange("p (g n) -> p g n", g=2), s5_small[:, 0:2, None].to_broadcast([32, 2, 64]))
                v.tensor_copy(s5row[0:16, 6, :].rearrange("p (g n) -> p g n", g=2),
                              s5_small[0:16, 2:4, None].to_broadcast([16, 2, 64])).then_inc(s["s5_step"], n.one("s5_step"))

            def s5_rows_b():
                dve.wait_ge(s["s5_exp"], n.due("s5_exp"))
                then(ts(row(13), s5_rows[:, 0, :], S5_MAX_REAL, None, MIN))
                tt(row(11), row(13), row(7), MULT)
                then(tt(row(12), s5_rows[:, 1, :], row(7), MULT))
                then(ts(row(8), row(12), 1 / (2 * np.pi), ROUND, MULT, ADD))
                then(ts(row(14), row(8), -ROUND, None, ADD))
                then(stt(row(8), row(14), -TWO_PI_HI, row(12), MULT, ADD))
                then(stt(row(8), row(14), -TWO_PI_LO, row(8), MULT, ADD))
                ts(row(8), row(8), PI_BELOW, -PI_BELOW, MIN, MAX).then_inc(s["s5_step"], n.one("s5_step"))
                then(ts(row(11), row(11), -87.0, None, MAX))
                then(ts(row(14), row(11), float(1 / np.log(2)), ROUND, MULT, ADD))
                then(ts(row(14), row(14), -ROUND, None, ADD))
                then(stt(row(11), row(14), -LN2_HI, row(11), MULT, ADD))
                then(stt(row(11), row(14), -LN2_LO, row(11), MULT, ADD))
                then(ts(row(0), row(11), 1 / 5040.0, None, MULT))
                for c in (1 / 720.0, 1 / 120.0, 1 / 24.0, 1 / 6.0, 0.5, 1.0):
                    then(stt(row(0), row(0), c, row(11), ADD, MULT))
                then(ts(row(0), row(0), 1.0, None, ADD))
                then(ts(row(14), row(14), 127.0, 2.0 ** 23, ADD, MULT))
                then(v.tensor_copy(row(15).bitcast(I32), row(14)))
                then(tt(row(0), row(0), row(15), MULT))

            def s5_rows_c():
                lr, li = row(13), s5_rows[:, 1, :]
                tt(row(14), lr, lr, MULT)
                then(tt(row(15), li, li, MULT))
                then(tt(row(14), row(14), row(15), ADD))
                then(v.reciprocal(row(14), row(14)))
                dve.wait_ge(s["s5_exp"], n.due("s5_exp"))
                tt(row(10), row(10), row(0), MULT)
                then(tt(row(9), row(9), row(0), MULT))
                then(ts(row(10), row(10), -1.0, None, ADD))
                tt(row(15), row(10), lr, MULT)
                tt(row(16), row(9), li, MULT)
                tt(row(17), row(10), li, MULT)
                then(tt(row(12), row(9), lr, MULT))
                tt(row(15), row(15), row(16), ADD)
                then(tt(row(17), row(17), row(12), SUB))
                then(tt(row(3), row(15), row(14), MULT))
                tt(row(4), row(17), row(14), MULT)
                ts(row(5), row(3), -1.0, None, MULT)
                then(ts(row(1).bitcast(F32R), row(8), 1 / (2 * np.pi), None, MULT))
                then(stt(row(2), row(1), -TWO_PI_HI, row(8), MULT, ADD))
                then(stt(row(2), row(1), -TWO_PI_LO, row(2), MULT, ADD))
                ts(row(2), row(2), 1 / (2 * np.pi), None, MULT).then_inc(s["s5_ready"], n.one("s5_ready"))

            def s5_masks(t):
                for r in range(2):
                    tt(mats_in[:, r, :].rearrange("p (q g c) -> p q g c", q=4, g=2),
                       b_raw[:, r, 4 * t:4 * t + 4, None, :].to_broadcast([P, 4, 2, 16]),
                       cst("bmask")[:, None, :, None].to_broadcast([P, 4, 2, 16]), MULT)
                    ins = tt(mats_in[:, 2 + r, :].rearrange("p (g n) -> p g n", g=2),
                             c_raw[:, r, t, None, :].to_broadcast([P, 2, 64]),
                             cst("cmask")[:, :, None].to_broadcast([P, 2, 64]), MULT)
                ins.then_inc(s["mats_masked"], n.one("mats_masked"))

            def s5_step(k):
                if k == 0:
                    s5_masks(0)
                if k % 4 == 3 and k < S5_PAIRS - 1:
                    dve.wait_ge(s["mats_psum"], n.due("mats_psum"))
                    s5_masks(k // 4 + 1)
                if 1 <= k <= S5_PAIRS:
                    q = k - 1
                    m = q % 3
                    dve.wait_ge(s["table_ready"], n.due("table_ready"))
                    if q:
                        dve.wait_ge(s["modulated"], n.due("modulated"))
                    dve.wait_ge(s["bu_done"], n.due("bu_done"))
                    bu = PS[:, 6 + q % 2, :].rearrange("p (r n) -> p r n", r=2)
                    tt(m1, bu, cos_t[:, m, None, :].to_broadcast([P, 2, T]), MULT)
                    tt(m2, bu, sin_t[:, m, None, :].to_broadcast([P, 2, T]), MULT).then_inc(s["bu_read"], n.one("bu_read"))
                if 2 <= k <= S5_PAIRS + 1:
                    q = k - 2
                    m, g = q % 3, g5[:, q % 2, :]
                    if q == S5_PAIRS - 1:
                        dve.wait_ge(s["modulated"], n.due("modulated"))
                    if q:
                        dve.wait_ge(s["h5_ready"], n.due("h5_ready"))
                    for i in range(2):
                        ins = v.tensor_tensor_scan(g[:, i * T:(i + 1) * T], s5c[:, 0, q:q + 1].to_broadcast([P, T]),
                                                   g[:, i * T:(i + 1) * T], 0.0, MULT, ADD)
                    then(ins)
                    g = g.rearrange("p (r n) -> p r n", r=2)
                    tt(damp_c, g, cos_t[:, m, None, :].to_broadcast([P, 2, T]), MULT)
                    tt(damp_s, g, sin_t[:, m, None, :].to_broadcast([P, 2, T]), MULT).then_inc(s["g_ready"], n.one("g_ready"))
                if k % 4 == 3 and k >= 7:
                    y5_add(k // 4 - 1)

            def y5_add(t):
                dve.wait_ge(s["y5_psum"], n.due("y5_psum", 4))
                stt(U5[:, t, :], U5[:, t, :], prm[:, 64 + t:65 + t], PS[:, 1 + t % 2, 0:T], MULT, ADD)\
                    .then_inc(s["y5_added"], n.one("y5_added"))

            def taps(i):
                dve.wait_ge(s["c_evicted"], n.due("c_evicted"))
                if i >= 2:
                    dve.wait_ge(s["silu_conv"], n.due("silu_conv"))
                for j in range(4):
                    for u in range(2):
                        t = 2 * i + u
                        x, y = conv_in[:, i % 2, u, j:j + T], conv_out[:, i % 2, u, :]
                        w = prm[:, 96 + 24 * j + t:97 + 24 * j + t]
                        if j == 0:
                            ins = ts(y, x, w, prm[:, 72 + t:73 + t], MULT, ADD)
                        else:
                            ins = stt(y, x, w, y, MULT, ADD)
                    if j < 3:
                        then(ins)
                ins.then_inc(s["tap_done"], n.one("tap_done"))

            def softplus_and_sums():
                e, u, dt, cum = (dt_rows[:, i, :] for i in (1, 2, 3, 4))
                dve.wait_ge(s["dt_act"], n.due("dt_act"))
                then(ts(cum, u, 1.0, None, EQ))
                then(stt(u, u, -1.0, cum, ADD, ADD))
                then(v.reciprocal(u, u))
                tt(u, u, dt, MULT)
                then(tt(cum, cum, e, MULT))
                then(tt(u, u, e, MULT))
                then(tt(u, u, cum, ADD))
                then(stt(dt, dt_rows[:, 0, :], 0.0, u, MAX, ADD))
                then(ts(u, dt, head_rows[:, 1:2], -1.0, MULT, MULT))
                for c in range(2):
                    ins = v.tensor_tensor_scan(cum[:, c * P:(c + 1) * P], cst("ones", 32), u[:, c * P:(c + 1) * P],
                                               0.0, MULT, ADD)
                then(ins)
                ts(e[:, 0:P], cum[:, 0:P], -1.0, cum[:, P - 1:P], MULT, ADD)\
                    .then_inc(s["dt_rows_ready"], n.one("dt_rows_ready"))

            def ssd_inputs(i):
                if i % 2 == 0:
                    dve.wait_ge(s["gm_psum"], n.due("gm_psum"))
                    tt(gmask[:, (i // 2) % 2, :], PS[:, 2, 0:384], cst("tri"), MULT)\
                        .then_inc(s["gm_ready"], n.one("gm_ready"))
                dve.wait_ge(s["xt_psum"], n.due("xt_psum"))
                for t in range(2):
                    ins = tt(xt[:, i % 2, t * T:(t + 1) * T].rearrange("p (h c) -> p h c", h=4),
                             PS[:, 3, t * T:(t + 1) * T].rearrange("p (h c) -> p h c", h=4),
                             dt_tok[:, t, 4 * i:4 * i + 4, None].to_broadcast([P, 4, 64]), MULT)
                ins.then_inc(s["xt_ready"], n.one("xt_ready"))

            def ssd_outputs(i):
                dve.wait_ge(s["c_evicted"], n.due("c_evicted"))
                for u in range(2):
                    t = 2 * i + u
                    dve.wait_ge(s["y_psum"], n.due("y_psum"))
                    then(stt(XC[:, t, :], XC[:, t, :], s5c[:, 6, t:t + 1], PS[:, 6 + u, 0:T], MULT, ADD))
                    tt(XC[:, t, :], XC[:, t, :], zbuf[i % 3][:, u, :], MULT).then_inc(s["y_ready"], n.one("y_ready"))

            def stage_a(i):
                if i % 2 == 0:
                    dve.wait_ge(s["group_root"], n.due("group_root"))
                    then(v.reciprocal(group_rstd[:, i // 2, :], group_rstd[:, i // 2, :]))
                if i >= 2:
                    wait_used(C_A + i - 2)
                for u in range(2):
                    t = 2 * i + u
                    stage_k(t % 4, lambda dst: stt(dst, XC[:, t, :], prm[:, 48 + t:49 + t],
                                                   group_rstd[:, i // 2, :], MULT, MULT))

            def split_inputs(src, c0):
                for i in range(5):
                    if i < 4:
                        if i >= 2:
                            wait_used(c0 + i - 2)
                        for u in range(2):
                            t = 2 * i + u
                            then(v.tensor_copy(k_hi[:, t % 4, :], src[:, t, :]))
                            tt(k_lo[:, t % 4, :], src[:, t, :], k_hi[:, t % 4, :].bitcast(F32), SUB)\
                                .then_inc(s["staged"], n.one("staged"))
                    if i:
                        convert((c0 + i - 1) % RING)

            def mixer():
                for k, (kind, i) in enumerate(TICKS):
                    if k == 0:
                        s5_rows_a()
                    if k == 1:
                        s5_rows_b()
                    if k == 2:
                        s5_rows_c()
                    if k == 4:
                        dve.wait_ge(s["s5_psum"], n.due("s5_psum"))
                        v.tensor_copy(s5c[:, 0:6, :], PS[:, 7, 0:192].rearrange("p (a n) -> p a n", a=6))
                        v.tensor_copy(s5c[:, 6, 0:16], PS[:, 7, 192:208]).then_inc(s["s5c_ready"], n.one("s5c_ready"))
                        dve.wait_ge(s["s5c_ready"], n.last("s5c_ready"))
                    if k == 5:
                        dve.wait_ge(s["c_evicted"], n.due("c_evicted", 5))
                        stt(dt_rows[:, 1, :], dt_rows[:, 0, :], -1.0, dt_rows[:, 0, :], MULT, MIN)\
                            .then_inc(s["dt_step"], n.one("dt_step"))
                    if k == 6:
                        dve.wait_ge(s["dt_act"], n.due("dt_act"))
                        ts(dt_rows[:, 2, :], dt_rows[:, 1, :], 1.0, None, ADD).then_inc(s["dt_step"], n.one("dt_step"))
                    if k == 7:
                        softplus_and_sums()
                    for q in S5_AT[k]:
                        s5_step(q)
                    if k == 25:
                        y5_add(7)
                    if 6 <= k < 18:
                        taps(k - 6)
                    if k == 25:
                        n.due("c_evicted", 8)
                        dve.wait_ge(s["dtok_psum"], n.due("dtok_psum"))
                        v.tensor_copy(dt_tok[:, :, :].rearrange("p a h -> p (a h)"), PS[:, 3, 0:160])\
                            .then_inc(s["dtok_ready"], n.one("dtok_ready"))
                    if kind == "z":
                        if i >= 1:
                            ssd_inputs(i - 1)
                        if i >= 2:
                            ssd_outputs(i - 2)
                    convert((MIX + k) % RING)
                ssd_inputs(7)
                ssd_outputs(6)
                ssd_outputs(7)
                n.due("silu_conv", 2)
                n.due("mats_psum")
                n.due("h5_ready")
                for i in range(8):
                    if i == 0:
                        stage_a(0)
                        low_parts(U5)
                    if i < 7:
                        stage_a(i + 1)
                    convert((C_A + i) % RING)
                wait_used(C_A + 7)
                tt(merged, ACC, G[:, 0:8, :], MULT).then_inc(s["acc_read"], n.one("acc_read"))
                for k, (kind, i) in enumerate(GLU_ORDER):
                    if kind == "g":
                        dve.wait_ge(s["c_evicted"], n.due("c_evicted", 2))
                        if i >= 2:
                            wait_used(C_G + GLU_ORDER.index(("b", i - 2)))
                        for u in range(2):
                            stage_k((2 * i + u) % 4, lambda dst: tt(dst, conv_out[:, i % 2, u, :],
                                                                    glu_gate[:, i % 2, u, :], MULT))
                    convert((C_G + k) % RING)
                wait_used(C_G + len(GLU_ORDER) - 1)
                then(tt(ACC, ACC, G[:, 8:16, :], MULT))
                tt(merged, merged, ACC, ADD).then_inc(s["acc_read"], n.one("acc_read"))
                dve.wait_ge(s["acc_read"], n.last("acc_read"))
                split_inputs(merged, C_OUT)

            v.memset(eps[:, 0:1], RMS_EPS)
            v.memset(eps[:, 1:2], HALF_PI)
            v.memset(eps[:, 2:3], LN_EPS)
            v.memset(conv_in[:, :, :, :], 0.0)
            v.memset(zero_bf[:, :], 0.0).then_inc(s["setup_done"], n.one("setup_done"))
            dve.sem_inc(s["weights_ready"], RING)
            n.given["weights_ready"] += RING
            dve.wait_ge(s["x_turned"], n.due("x_turned"))
            v.tensor_copy(H[:, :, :].rearrange("p k n -> p (k n)"), ACC_FLAT).then_inc(s["h_ready"], n.one("h_ready"))
            n.due("chunk_used", RING)
            for slot in range(RING):
                convert(slot)
                n.due("chunk_used", -1)
            with n.loop(dve, DEPTH, "layer"):
                pos[0] = -1
                pre_norm(0)
                ffn()
                post_norm(8, 0.5)
                pre_norm(16)
                mixer()
                post_norm(24, 1.0)
                pre_norm(32)
                ffn()
                post_norm(40, 0.5)


            pos[0] = -1

            def then_on(ins, event):
                ins.then_inc(s[event], n.one(event))
                dve.wait_ge(s[event], n.last(event))

            def layer_norm(src, g0, b0, split=True):
                stt(H[:, :, :], H[:, :, :], ALPHA, src, MULT, ADD).then_inc(s["h_ready"], n.one("h_ready"))
                dve.wait_ge(s["h_ready"], n.last("h_ready"))
                dve.wait_ge(s["mean_sum"], n.due("mean_sum"))
                stt(H[:, :, :], PS[:, 4, None, 0:T].to_broadcast([P, DT, T]), -1.0 / D, H[:, :, :], MULT, ADD)\
                    .then_inc(s["centered"], n.one("centered"))
                dve.wait_ge(s["centered"], n.last("centered"))
                dve.wait_ge(s["rooted"], n.due("rooted"))
                then(v.reciprocal(rstd[:, :], rstd[:, :]))
                for i in range(2):
                    for k in range(4 * i, 4 * i + 4):
                        ins = stt(H[:, k, :], H[:, k, :], prm[:, g0 + k:g0 + k + 1], rstd[:, :], MULT, MULT)
                    then(ins)
                    for k in range(4 * i, 4 * i + 4):
                        ins = ts(H[:, k, :], H[:, k, :], prm[:, b0 + k:b0 + k + 1], None, ADD)
                    if split:
                        ins.then_inc(s["xf_ready"], n.one("xf_ready"))
                    elif i:
                        ins.then_inc(s["normed"], n.one("normed"))
                if split:
                    low_parts(H)

            def attention(heads):
                for i in range(len(heads) + 1):
                    if i < len(heads):
                        b = i % 2
                        dve.wait_ge(s["att_scores"], n.due("att_scores"))
                        if i >= 2:
                            dve.wait_ge(s["att_turned"], n.due("att_turned"))
                        scores = PS[:, b, :].rearrange("p (t n) -> p t n", t=2)
                        if heads[i][5]:
                            then(tt(probs[:, b], scores, causal, ADD))
                            scores = probs[:, b]
                        then(v.tensor_reduce(att_small[:, b, 0:2], scores, AX_X, MAX))
                        ts(att_small[:, b, 2:4], att_small[:, b, 0:2], -ATTN_SCALE, None, MULT)\
                            .then_inc(s["att_max"], n.one("att_max"))
                    if i:
                        b = (i - 1) % 2
                        dve.wait_ge(s["att_exp"], n.due("att_exp"))
                        then(v.reciprocal(att_small[:, b, 0:2], att_small[:, b, 4:6]))
                        for t in range(2):
                            ins = ts(probs[:, b, t, :], probs[:, b, t, :], att_small[:, b, t:t + 1], None, MULT)
                        ins.then_inc(s["att_norm"], n.one("att_norm"))
                n.due("att_turned", 2)
                dve.wait_ge(s["att_evicted"], n.due("att_evicted", len(heads) // 2))

            dve.wait_ge(s["x_turned"], n.due("x_turned"))
            for i in range(2):
                v.tensor_copy(squares[:, 4 * i:4 * i + 4, :], ACC[:, 4 * i:4 * i + 4, :])\
                    .then_inc(s["xf_ready"], n.one("xf_ready"))
            low_parts(squares)
            dve.wait_ge(s["x_ready"], n.last("x_ready"))
            dve.wait_ge(s["params2_in"], n.due("params2_in", 16 * 8))
            then(v.tensor_copy(rope_a, positions.bitcast(I32)))
            then(ts(rope_a, rope_a, cst("freq"), None, MULT))
            then(ts(rope_b, rope_a, 1 / (2 * np.pi), ROUND, MULT, ADD))
            then(ts(rope_b, rope_b, -ROUND, None, ADD))
            then(stt(rope_a, rope_b, -TWO_PI_HI, rope_a, MULT, ADD))
            then(stt(rope_a, rope_b, -TWO_PI_LO, rope_a, MULT, ADD))
            ts(rope_a, rope_a, PI_BELOW, -PI_BELOW, MIN, MAX).then_inc(s["rope_ang"], n.one("rope_ang"))
            then(v.memset(gated[:, :, 0:2], 0.0))
            for c in range(4):
                if c == 3:
                    low_parts(H)
                convert((B_MEM + c) % RING)
            dve.wait_ge(s["prm_ready"], n.due("prm_ready"))
            n.due("c_evicted", 4 + 6)
            for i in range(10):
                if i >= 7:
                    dve.wait_ge(s["c_evicted"], n.due("c_evicted"))
                    for t in (2 * i - 14, 2 * i - 13):
                        ins = tt(gated[:, t, 2:T + 2], XC[:, 6 + t, :], XC[:, 12 + t, :], MULT)
                    then(ins)
                    for w in range(3):
                        for t in (2 * i - 14, 2 * i - 13):
                            tap = prm[:, 64 + 6 * w + t:65 + 6 * w + t]
                            if w == 0:
                                ins = ts(tapped[:, t, :], gated[:, t, 0:T], tap, None, MULT)
                            else:
                                ins = stt(tapped[:, t, :], gated[:, t, w:w + T], tap, tapped[:, t, :], MULT, ADD)
                        then(ins)
                    for t in (2 * i - 14, 2 * i - 13):
                        ins = tt(XC[:, t, :], XC[:, t, :], tapped[:, t, :], MULT)
                convert((B_INA + i) % RING)
            then(ins)
            n.due("c_evicted")
            attention(heads_a)
            split_inputs(XC, B_WO1)
            wait_used(B_WO1 + 3)
            layer_norm(ACC, 0, 16)
            ffn()
            layer_norm(ACC, 32, 48)
            for i in range(10):
                convert((B_KV + i) % RING)
            dve.wait_ge(s["rope_table"], n.due("rope_table"))
            for i, t in enumerate(rope_tiles):
                dve.wait_ge(s["rope_psum"], n.due("rope_psum"))
                tt(rope_a, XC[:, t, :], rope_cos, MULT)
                then(tt(rope_b, PS[:, 6 + i % 2, 0:T], rope_sin, MULT))
                then_on(tt(XC[:, t, :], rope_a, rope_b, ADD), "roped")
            attention(heads_b)
            split_inputs(XC, B_WO2)
            wait_used(B_WO2 + 3)
            layer_norm(ACC, 8, 24, split=False)
            first = cst("first")[:, None, :].to_broadcast([P, 2, N_EXPERTS])

            def small(i):
                return rsm[:, i, :]

            def wide(i):
                return rsm[:, i, :, None].to_broadcast([P, 2, N_EXPERTS])

            def top(values, i, dst):
                then(v.tensor_reduce(small(i), values, AX_X, MAX))
                then(tt(dst, values, wide(i), EQ))
                then(tt(dst, dst, first, MULT))
                then(v.tensor_reduce(small(i + 1), dst, AX_X, MAX))
                then(tt(dst, first, wide(i + 1), EQ))

            dve.wait_ge(s["logits"], n.due("logits"))
            then(v.tensor_copy(lg, PS[:, 4, 0:16].rearrange("p (t e) -> p t e", t=2)))
            top(lg, 0, top1)
            then(stt(rest, top1, -1e30, lg, MULT, ADD))
            top(rest, 2, top2)
            tt(small(4), small(2), small(0), SUB).then_inc(s["gate_diff"], n.one("gate_diff"))
            then_on(tt(chosen, top1, top2, ADD), "masks_ready")
            dve.wait_ge(s["route_exp"], n.due("route_exp"))
            then(ts(small(6), small(5), 1.0, None, ADD))
            then(v.reciprocal(small(6), small(6)))
            then(tt(small(7), small(6), small(5), MULT))
            tt(top1, top1, wide(6), MULT)
            then(tt(top2, top2, wide(7), MULT))
            then(tt(gate_of[:, :, 0:N_EXPERTS], top1, top2, ADD))
            dve.wait_ge(s["ranks"], n.due("ranks"))
            then(stt(slot_of[:, :, 0:N_EXPERTS], chosen, -1000.0, PS[:, 5, 0:16].rearrange("p (t e) -> p t e", t=2), MULT, ADD))
            then(ts(slot_of[:, :, 0:N_EXPERTS], slot_of[:, :, 0:N_EXPERTS], 1000.0, None, ADD))
            ts(slot_of[:, :, N_EXPERTS:], slot_of[:, :, 0:1], -float(SLOTS), None, ADD)
            v.tensor_copy(gate_of[:, :, N_EXPERTS:], gate_of[:, :, 0:1])
            v.memset(moe_sum[:, :, :], 0.0)
            then(v.tensor_reduce(small(8)[:, 0:1], PS[:, 5, 16:24], AX_X, MAX))
            then(ts(small(8)[:, 0:1], small(8)[:, 0:1], float(SLOTS), 1.0, ALU.is_gt, ADD))
            then_on(v.tensor_copy(n_pass.bitcast(I32), small(8)[:, 0:1]), "routed")
            passes = dve.value_load(n_pass[0:1, :].bitcast(I32), min_val=1, max_val=2)

            def make_pick(e):
                v.tensor_copy(cur[:, 0:2, None], slot_of[:, :, e])
                then(v.tensor_copy(cur[:, 2:4, None], gate_of[:, :, e]))
                for t in range(2):
                    ts(pick[:, t, :], cst("iota", P, 0, P), cur[:, t:t + 1], None, EQ)
                    ins = ts(pick[:, 2 + t, :], cst("iota", P, 0, P), cur[:, t:t + 1], cur[:, 2 + t:3 + t], EQ, MULT)
                ins.then_inc(s["picked"], n.one("picked"))

            def expert_inputs():
                for i in range(2):
                    dve.wait_ge(s["xh_ready"], n.due("xh_ready"))
                    tt(x_lo[:, 4 * i:4 * i + 4, 0:P], PS[:, 2 + i, :].rearrange("p (k n) -> p k n", n=P),
                       x_hi[:, 4 * i:4 * i + 4, 0:P].bitcast(F32), SUB).then_inc(s["x_ready"], n.one("x_ready"))

            make_pick(slice(0, 1))
            expert_inputs()
            dve.sem_inc(s["sum_added"], 2)
            n.given["sum_added"] += 2
            with n.loop(dve, passes, "pass"):
                with n.loop(dve, N_EXPERTS, "expert") as e:
                    dve.wait_ge(s["scatter_turned"], n.due("scatter_turned"))
                    make_pick(bass.ds(e + 1, 1))
                    with n.loop(dve, STEPS, "moe_step"):
                        dve.wait_ge(s["silu_done"], n.due("silu_done"))
                        wait_used(pos[0] + 2)
                        tt(stage[:, 0, :], act_out[:, 0, :], PS[:, 5, 0:T], MULT)                            .then_inc(s["hidden_ready"], n.one("hidden_ready"))
                        dve.wait_ge(s["kh_ready"], n.due("kh_ready"))
                        tt(k_lo[:, 0:2, 0:P], PS[:, 6, 0:T].rearrange("p (k n) -> p k n", n=P),
                           k_hi[:, 0:2, 0:P].bitcast(F32), SUB).then_inc(s["staged"], n.one("staged"))
                        for slot in MOE_SLOTS:
                            convert(slot)
                    expert_inputs()
                    for i, b in enumerate((6, 2)):
                        dve.wait_ge(s["scattered"], n.due("scattered"))
                        half = moe_sum[:, 4 * i:4 * i + 4, :]
                        tt(half, half, PS[:, b:b + 2, :].rearrange("p b (u n) -> p (b u) n", u=2), ADD)\
                            .then_inc(s["sum_added"], n.one("sum_added"))
                    dve.wait_ge(s["sum_added"], n.last("sum_added"))
                then(ts(slot_of, slot_of, -float(SLOTS), None, ADD))
            layer_norm(moe_sum[:, :, :], 40, 56, split=False)

        @block.gpsimd
        def _(pool):
            n = Count()
            g = nc.gpsimd
            tt, ts = g.tensor_tensor, g.tensor_scalar


            def then(ins):
                ins.then_inc(s["pool_step"], n.one("pool_step"))
                pool.wait_ge(s["pool_step"], n.last("pool_step"))

            def alone():
                pool.sem_inc(s["pool_waited"], 1)

            def s5_turns(q):
                if q:
                    pool.wait_ge(s["table_ready"], n.due("table_ready"))
                x, lo, k = (turns[:, i, :] for i in range(3))
                tt(x, cst("iota"), s5c[:, 1, q:q + 1].to_broadcast([P, T]), MULT)
                then(ts(lo, cst("iota"), s5c[:, 2, q:q + 1], None, MULT))
                then(tt(k, x, lo, ADD))
                alone()
                then(ts(k, k, ROUND, -ROUND, ADD, ADD))
                then(tt(x, x, k, SUB))
                then(tt(x, x, lo, ADD))
                alone()
                ts(x, x, 0.5, -0.5, MIN, MAX).then_inc(s["turns_ready"], n.one("turns_ready"))

            def s5_cproj(t):
                pool.wait_ge(s["mats_ready"], n.due("mats_ready"))
                co = cproj[:, t % 2, :].rearrange("p (r n) -> p r n", r=2)
                q4 = lambda x: x.rearrange("p (q c) -> p q c", q=4)
                coef = lambda i: s5c[:, i, 4 * t:4 * t + 4, None].to_broadcast([P, 4, 32])
                cre, cim = q4(mats[:, 2, :]), q4(mats[:, 3, :])
                tt(q4(co[:, 0, :]), cre, coef(3), MULT)
                then(tt(q4(cpt[:, 0, :]), cim, coef(4), MULT))
                then(tt(co[:, 0, :], co[:, 0, :], cpt[:, 0, :], ADD))
                tt(q4(co[:, 1, :]), cre, coef(4), MULT)
                then(tt(q4(cpt[:, 1, :]), cim, coef(5), MULT))
                tt(co[:, 1, :], co[:, 1, :], cpt[:, 1, :], ADD).then_inc(s["cproj_ready"], n.one("cproj_ready"))

            def s5_step(k):
                if k < S5_PAIRS:
                    s5_turns(k)
                if k % 4 == 1 and k < S5_PAIRS:
                    s5_cproj(k // 4)
                if 1 <= k <= S5_PAIRS:
                    q = k - 1
                    pool.wait_ge(s["bu_read"], n.due("bu_read"))
                    o = g5[:, q % 2, :]
                    tt(o[:, 0:T], m1[:, 0, :], m2[:, 1, :], ADD)
                    tt(o[:, T:2 * T], m1[:, 1, :], m2[:, 0, :], SUB).then_inc(s["modulated"], n.one("modulated"))
                if 2 <= k <= S5_PAIRS + 1:
                    q = k - 2
                    pool.wait_ge(s["g_ready"], n.due("g_ready"))
                    if q:
                        pool.wait_ge(s["y5_psum"], n.due("y5_psum"))
                    tt(h5[:, 0, :], damp_c[:, 0, :], damp_s[:, 1, :], SUB)
                    tt(h5[:, 1, :], damp_c[:, 1, :], damp_s[:, 0, :], ADD).then_inc(s["h5_ready"], n.one("h5_ready"))

            def ssd_masks(i):
                if i % 2 == 0:
                    pool.wait_ge(s["gm_ready"], n.due("gm_ready"))
                for h in range(4):
                    pool.wait_ge(s["decay_ready"], n.due("decay_ready"))
                    d = decay[:, i % 2, h, :]
                    tt(d, d, gmask[:, (i // 2) % 2, :], MULT).then_inc(s["masked"], n.one("masked"))

            with n.loop(pool, DEPTH, "layer"):
                pool.wait_ge(s["s5c_ready"], n.due("s5c_ready"))
                for k in range(S5_STEPS):
                    s5_step(k)
                n.due("table_ready")
                n.due("y5_psum")
                for i in range(8):
                    ssd_masks(i)


_INS = ["x", "ffn1_pre_g", "ffn1_post_g", "ffn1_w_gate", "ffn1_w_up", "ffn1_w_down", "mix_pre_g", "mix_post_g",
        "w_in", "ssd_conv_w", "ssd_conv_b", "ssd_dt_bias", "ssd_a_log", "ssd_d", "ssd_norm_g", "w_branch_a",
        "s5_lambda_re", "s5_lambda_im", "s5_b_re", "s5_b_im", "s5_c_re", "s5_c_im", "s5_log_step", "s5_d", "s5_w_glu",
        "w_branch_b", "w_out", "ffn2_pre_g", "ffn2_post_g", "ffn2_w_gate", "ffn2_w_up", "ffn2_w_down", "mem_2",
        "positions_2", "w_in_a_2", "conv_a_2", "w_q_b_2", "w_kv_shared_2", "w_mem_kv_2", "w_o_2", "ln1_g_2",
        "ln1_b_2", "ln2_g_2", "ln2_b_2", "w_gu_dense_2", "w_down_dense_2", "w_router_2", "w_gu_moe_2",
        "w_down_moe_2"]


def kernel(**inputs):
    import numpy as _np
    import concourse.bacc as _bacc
    from concourse import mybir as _mybir
    from concourse.bass_utils import run_bass_kernel_spmd as _run

    nc = _bacc.Bacc("TRN2", target_bir_lowering=False, num_devices=1)
    arrays = {name: _np.ascontiguousarray(inputs[name]) for name in _INS}
    arrays["consts"] = constants()
    arrays["causal"] = causal_mask()
    a = {name: nc.dram_tensor(f"in_{name}_dram", v.shape, _mybir.dt.from_np(v.dtype), kind="ExternalInput").ap()
         for name, v in arrays.items()}
    out = nc.dram_tensor("out_0_dram", (1, T, D), _mybir.dt.float32, kind="ExternalOutput").ap()
    build(nc, a, out)
    r = _run(nc, [{f"in_{name}_dram": v for name, v in arrays.items()}], core_ids=[0])
    return r.results[0]["out_0_dram"]
```
